# Optimizing a Trainium2 kernel written in Bass

```python
import math
import jax, jax.numpy as jnp
from jax import lax
import numpy as np

D_MODEL = 1024
BATCH = 1
SEQ = 4096
DEPTH = 2

N_MIXERS = 2
N_SSM_LAYERS = (DEPTH + 1) // 2
N_CONV_LAYERS = DEPTH // 2
SSM_WIDTH = D_MODEL
SSM_GROUP = 16
SSM_GROUPS = SSM_WIDTH // SSM_GROUP
SSM_STATE = 64
SSM_CHUNK = 128
DT_MIN = 0.001
DT_MAX = 0.1
CONV_WIDTH = D_MODEL
CONV_K = 3
N_GROUPS = 4
EXPERTS_PER_GROUP = 8
N_EXPERTS = N_GROUPS * EXPERTS_PER_GROUP
TOP_K = 2
D_EXPERT = D_MODEL // 2
RMS_EPS = 1e-6

kernel_name = 'hybrid_s5_shortconv_hier_moe'

def rmsnorm(x, g):
    x32 = x.astype(jnp.float32)
    y = x32 * lax.rsqrt(jnp.mean(x32 * x32, axis=-1, keepdims=True) + RMS_EPS)
    return (y * g.astype(jnp.float32)).astype(x.dtype)

def modulate(h, shift, scale):
    return h * (1 + scale[:, None, :]) + shift[:, None, :]

def _complex_affine_combine(e1, e2):
    a1r, a1i, b1r, b1i = e1
    a2r, a2i, b2r, b2i = e2
    return (a2r * a1r - a2i * a1i,
            a2r * a1i + a2i * a1r,
            a2r * b1r - a2i * b1i + b2r,
            a2r * b1i + a2i * b1r + b2i)

def s5_mixer(h, w_in, lam_re, lam_im, log_dt, b_re, b_im, c_re, c_im, d_skip, w_glu):
    f32 = jnp.float32
    bsz, seq, _ = h.shape
    u = (h @ w_in).astype(f32)
    lr, li = lam_re.astype(f32), lam_im.astype(f32)
    dt = jnp.exp(log_dt.astype(f32))[:, None]
    mag = jnp.exp(lr * dt)
    ab_re = mag * jnp.cos(li * dt)
    ab_im = mag * jnp.sin(li * dt)
    den = lr * lr + li * li
    cf_re = ((ab_re - 1) * lr + ab_im * li) / den
    cf_im = (ab_im * lr - (ab_re - 1) * li) / den
    br, bi = b_re.astype(f32), b_im.astype(f32)
    bb_re = cf_re[..., None] * br - cf_im[..., None] * bi
    bb_im = cf_re[..., None] * bi + cf_im[..., None] * br
    cr, ci = c_re.astype(f32), c_im.astype(f32)
    n_chunks = seq // SSM_CHUNK
    uc = u.reshape(bsz, n_chunks, SSM_CHUNK, SSM_GROUPS, SSM_GROUP).transpose(1, 0, 2, 3, 4)
    blk_shape = (bsz, SSM_CHUNK, SSM_GROUPS, SSM_STATE)
    a_re = jnp.broadcast_to(ab_re, blk_shape)
    a_im = jnp.broadcast_to(ab_im, blk_shape)

    def chunk_step(carry, u_blk):
        h_re, h_im = carry
        bu_re = jnp.einsum('btgk,gpk->btgp', u_blk, bb_re)
        bu_im = jnp.einsum('btgk,gpk->btgp', u_blk, bb_im)
        A_re, A_im, S_re, S_im = lax.associative_scan(
            _complex_affine_combine, (a_re, a_im, bu_re, bu_im), axis=1)
        st_re = S_re + A_re * h_re[:, None] - A_im * h_im[:, None]
        st_im = S_im + A_re * h_im[:, None] + A_im * h_re[:, None]
        y = (jnp.einsum('btgp,gkp->btgk', st_re, cr)
             - jnp.einsum('btgp,gkp->btgk', st_im, ci))
        return (st_re[:, -1], st_im[:, -1]), y

    h0 = jnp.zeros((bsz, SSM_GROUPS, SSM_STATE), f32)
    _, ys = lax.scan(chunk_step, (h0, h0), uc)
    y = ys.transpose(1, 0, 2, 3, 4).reshape(bsz, seq, SSM_WIDTH) + d_skip.astype(f32) * u
    y = jax.nn.gelu(y).astype(h.dtype)
    val, gate = jnp.split(y @ w_glu, 2, axis=-1)
    return val * jax.nn.sigmoid(gate)

def short_conv_mixer(h, w_in, conv_w, w_out):
    b_g, c_g, v = jnp.split(h @ w_in, 3, axis=-1)
    u = c_g * v
    z = lax.conv_general_dilated(
        u, conv_w[:, None, :].astype(u.dtype), window_strides=(1,),
        padding=[(CONV_K - 1, 0)], dimension_numbers=('NWC', 'WIO', 'NWC'),
        feature_group_count=CONV_WIDTH)
    return (b_g * z) @ w_out

def hier_moe(h, wg, bg, we, be, w1, w3, w2):
    f32 = jnp.float32
    bsz, seq, d = h.shape
    T = bsz * seq
    hf = h.reshape(T, d)
    g_prob = jax.nn.softmax((hf @ wg).astype(f32) + bg.astype(f32), axis=-1)
    gp, gi = lax.top_k(g_prob, 1)
    e_logits = ((hf @ we).astype(f32) + be.astype(f32)).reshape(T, N_GROUPS, EXPERTS_PER_GROUP)
    e_sel = jnp.take_along_axis(e_logits, gi[:, :, None], axis=1)[:, 0]
    ev, ei = lax.top_k(e_sel, TOP_K)
    wts = gp * jax.nn.softmax(ev, axis=-1)
    eid = gi * EXPERTS_PER_GROUP + ei
    flat_e = eid.reshape(-1)
    order = jnp.argsort(flat_e)
    tok = order // TOP_K
    sizes = jnp.bincount(flat_e, length=N_EXPERTS).astype(jnp.int32)
    xs = hf[tok]
    a = lax.ragged_dot(xs, w1, sizes)
    b = lax.ragged_dot(xs, w3, sizes)
    o = lax.ragged_dot(jax.nn.silu(a) * b, w2, sizes)
    o = o * wts.reshape(-1)[order][:, None].astype(o.dtype)
    y = jnp.zeros_like(hf).at[tok].add(o)
    return y.reshape(bsz, seq, d)

def setup_inputs(seed: int = 0) -> dict:
    f32 = jnp.float32
    key = jax.random.key(seed)
    ks = jax.random.split(key, 32)

    def nrm(k, shape, scale):
        return jax.random.normal(k, shape, f32) * scale

    n_idx = jnp.arange(SSM_STATE, dtype=f32)
    ssm_shape = (N_SSM_LAYERS, SSM_GROUPS, SSM_STATE)
    return {
        'x': nrm(ks[0], (BATCH, SEQ, D_MODEL), 1.0),
        'c': nrm(ks[1], (BATCH, D_MODEL), 1.0),
        'ada_w': nrm(ks[2], (DEPTH, D_MODEL, 6 * D_MODEL), 0.1 * D_MODEL ** -0.5),
        'ada_b': nrm(ks[3], (DEPTH, 6 * D_MODEL), 0.02),
        'norm1_g': 1.0 + nrm(ks[4], (DEPTH, D_MODEL), 0.02),
        'norm2_g': 1.0 + nrm(ks[5], (DEPTH, D_MODEL), 0.02),
        'ssm_w_in': nrm(ks[6], (N_SSM_LAYERS, D_MODEL, SSM_WIDTH), D_MODEL ** -0.5),
        'ssm_lam_re': -0.5 + nrm(ks[7], ssm_shape, 0.01),
        'ssm_lam_im': math.pi * n_idx + nrm(ks[8], ssm_shape, 0.01),
        'ssm_log_dt': jax.random.uniform(ks[9], (N_SSM_LAYERS, SSM_GROUPS), f32,
                                         math.log(DT_MIN), math.log(DT_MAX)),
        'ssm_b_re': nrm(ks[10], (N_SSM_LAYERS, SSM_GROUPS, SSM_STATE, SSM_GROUP), (2 * SSM_GROUP) ** -0.5),
        'ssm_b_im': nrm(ks[11], (N_SSM_LAYERS, SSM_GROUPS, SSM_STATE, SSM_GROUP), (2 * SSM_GROUP) ** -0.5),
        'ssm_c_re': nrm(ks[12], (N_SSM_LAYERS, SSM_GROUPS, SSM_GROUP, SSM_STATE), SSM_STATE ** -0.5),
        'ssm_c_im': nrm(ks[13], (N_SSM_LAYERS, SSM_GROUPS, SSM_GROUP, SSM_STATE), SSM_STATE ** -0.5),
        'ssm_d': nrm(ks[14], (N_SSM_LAYERS, SSM_WIDTH), 1.0),
        'ssm_w_glu': nrm(ks[15], (N_SSM_LAYERS, SSM_WIDTH, 2 * D_MODEL), SSM_WIDTH ** -0.5),
        'conv_w_in': nrm(ks[16], (N_CONV_LAYERS, D_MODEL, 3 * CONV_WIDTH), D_MODEL ** -0.5),
        'conv_w': nrm(ks[17], (N_CONV_LAYERS, CONV_K, CONV_WIDTH), CONV_K ** -0.5),
        'conv_w_out': nrm(ks[18], (N_CONV_LAYERS, CONV_WIDTH, D_MODEL), CONV_WIDTH ** -0.5),
        'moe_wg': nrm(ks[19], (DEPTH, D_MODEL, N_GROUPS), D_MODEL ** -0.5),
        'moe_bg': nrm(ks[20], (DEPTH, N_GROUPS), 0.01),
        'moe_we': nrm(ks[21], (DEPTH, D_MODEL, N_EXPERTS), D_MODEL ** -0.5),
        'moe_be': nrm(ks[22], (DEPTH, N_EXPERTS), 0.01),
        'moe_w1': nrm(ks[23], (DEPTH, N_EXPERTS, D_MODEL, D_EXPERT), D_MODEL ** -0.5),
        'moe_w3': nrm(ks[24], (DEPTH, N_EXPERTS, D_MODEL, D_EXPERT), D_MODEL ** -0.5),
        'moe_w2': nrm(ks[25], (DEPTH, N_EXPERTS, D_EXPERT, D_MODEL), D_EXPERT ** -0.5),
        'final_g': 1.0 + nrm(ks[26], (D_MODEL,), 0.02),
    }

def reference(x, c, ada_w, ada_b, norm1_g, norm2_g,
              ssm_w_in, ssm_lam_re, ssm_lam_im, ssm_log_dt, ssm_b_re, ssm_b_im,
              ssm_c_re, ssm_c_im, ssm_d, ssm_w_glu,
              conv_w_in, conv_w, conv_w_out,
              moe_wg, moe_bg, moe_we, moe_be, moe_w1, moe_w3, moe_w2, final_g):
    cond = jax.nn.silu(c)
    for i in range(DEPTH):
        mod = cond @ ada_w[i] + ada_b[i]
        sh1, sc1, g1, sh2, sc2, g2 = jnp.split(mod, 6, axis=-1)
        hn = modulate(rmsnorm(x, norm1_g[i]), sh1, sc1)
        j = i // N_MIXERS
        if i % N_MIXERS == 0:
            out = s5_mixer(hn, ssm_w_in[j], ssm_lam_re[j], ssm_lam_im[j], ssm_log_dt[j],
                           ssm_b_re[j], ssm_b_im[j], ssm_c_re[j], ssm_c_im[j],
                           ssm_d[j], ssm_w_glu[j])
        else:
            out = short_conv_mixer(hn, conv_w_in[j], conv_w[j], conv_w_out[j])
        x = x + (1 + g1)[:, None, :] * out
        hn = modulate(rmsnorm(x, norm2_g[i]), sh2, sc2)
        x = x + (1 + g2)[:, None, :] * hier_moe(hn, moe_wg[i], moe_bg[i], moe_we[i], moe_be[i],
                                                moe_w1[i], moe_w3[i], moe_w2[i])
    return rmsnorm(x, final_g)


_drawn_inputs = setup_inputs


def setup_inputs(seed=0):
    import zlib

    import numpy as np

    out = dict(_drawn_inputs(seed))
    spreads = {}
    factors = {}
    for name, (base, spread) in spreads.items():
        noise = np.random.default_rng([zlib.crc32(name.encode()), seed]).standard_normal(out[name].shape)
        drawn = base * np.exp(spread * noise) if base else spread * noise
        out[name] = __import__('jax').numpy.asarray(drawn.astype(out[name].dtype))
    for name, factor in factors.items():
        out[name] = (out[name] * factor).astype(out[name].dtype)
    return out
```

```python
from contextlib import ExitStack

import numpy as np
import concourse.bass as bass
from concourse import mybir

F32 = mybir.dt.float32
F32R = mybir.dt.float32r
I32 = mybir.dt.int32
ALU = mybir.AluOpType
ACT = mybir.ActivationFunctionType
AX = mybir.AxisListType

P = 128
D = 1024
KD = D // P
T = 4096
NT = T // P
HALF = 512
L = T // P
G, S, CH = 64, 64, 16
KB = L * CH // P
SB = L // KB
LEVELS = 7
NG, EG, NE = 4, 8, 32
FE = 512
KF = FE // P
TILES = 2 * T // P + NE - 1
SLOTS = (TILES + 1) * P
EPS = 1e-6
MOD = 6 * D
SH1, SC1, G1, SH2, SC2, G2 = range(6)


class Chain:

    def __init__(self, eng, sem, base=0):
        self.eng, self.sem, self.base, self.n = eng, sem, base, 0

    def __call__(self, ins):
        self.n += 1
        ins.then_inc(self.sem, 1)
        self.eng.wait_ge(self.sem, self.base + self.n)


def at(i, s, d=0):
    return i + (s + d) // 2, (s + d) % 2


def pairs(eng, n, body):
    body(0, True, False)
    with eng.Fori(1, n - 1) as i:
        body(i, False, False)
    body(n - 1, False, True)


class Core:

    def __init__(self, nc, ctx):
        self.nc, self.ctx = nc, ctx

    def sem(self, name, n=None):
        if n is None:
            return self.nc.alloc_semaphore(name)
        return [self.nc.alloc_semaphore(f"{name}{i}") for i in range(n)]

    def phase(self, build, *args, **kw):
        with self.nc.cleanup_on_exit():
            build(self, *args, **kw)

    def sb(self, ctx, name, shape, dt=F32):
        return ctx.enter_context(self.nc.sbuf_tensor(name, shape, dt))

    def sbs(self, ctx, name, n, shape, dt=F32):
        return [self.sb(ctx, f"{name}{i}", shape, dt) for i in range(n)]

    def raw_low(self, ctx, name, shape):
        at_byte = -(-self.nc.sbuf_base // 32) * 32
        raw = self.sb(ctx, name + "_raw", shape)
        return raw, self.nc.alloc_sbuf_tensor_at(name + "_lo", shape, F32R, offset=at_byte)

    def ps(self, ctx, name, shape):
        return ctx.enter_context(self.nc.psum_tensor(name, shape, F32))


def product(pe, out, lhs, rhs, start, stop):
    (lh, ll), (rh, rl) = lhs, rhs
    pe.matmul(out, lh, rl, start=start, stop=False)
    pe.matmul(out, ll, rh, start=False, stop=False)
    return pe.matmul(out, lh, rh, start=False, stop=stop)


def row(ap, a, n):
    return ap[:, a:a + n].broadcast_to([P, n])



def constants(core, ident):
    nc = core.nc
    step = core.sem("ident_step")
    with nc.Block() as block:
        @block.gpsimd
        def _(pool):
            c = Chain(pool, step)
            c(pool.memset(ident[:], 0.0))
            c(pool.affine_select(out=ident[:], in_=ident[:], compare_op=ALU.not_equal, fill=1.0,
                                 base=0, pattern=[[-1, P]], channel_multiplier=1))


def modulation(core, c_in, ada_w, ada_b, mod_dram):
    nc = core.nc
    chunks = MOD // HALF
    c_ld, b_ld, w_ld = core.sem("c_loaded"), core.sem("ada_b_loaded"), core.sem("ada_w_loaded", 2)
    cond_ready, mm, free = core.sem("cond_ready"), core.sem("mod_product", 2), core.sem("mod_psum_free", 2)
    done, st = core.sem("mod_done"), core.sem("mod_stored")
    w_view = ada_w.rearrange("l (k p) n -> l p k n", p=P)
    with ExitStack() as ctx:
        cond = core.sb(ctx, "cond", [P, 2, KD])
        w = core.sbs(ctx, "ada_w", 2, [P, KD, HALF])
        bias = core.sb(ctx, "ada_b_row", [1, 2, MOD])
        mod = core.sb(ctx, "mod_row", [1, 2, MOD])
        ps = [core.ps(ctx, f"mod_ps{l}", [P, HALF]) for l in range(2)]
        block = ctx.enter_context(nc.Block())

        @block.sync
        def _(sp):
            sp.dma_start(cond[:, 0, :], c_in.rearrange("b (k p) -> p (b k)", p=P),
                         allow_slow_non_contiguous=True).then_inc(c_ld, 16)
            sp.dma_start(bias[:], ada_b.rearrange("(a l) n -> a l n", a=1)).then_inc(b_ld, 16)
            with sp.Fori(0, chunks) as n:
                for l in range(2):
                    sp.wait_ge(mm[l], n + 1)
                    sp.dma_start(w[l][:], w_view[l, :, :, bass.ts(n, HALF)]).then_inc(w_ld[l], 16)
            sp.wait_ge(done, 2 * chunks)
            sp.dma_start(mod_dram.rearrange("(a l) n -> a l n", a=1), mod[:]).then_inc(st, 16)
            sp.wait_ge(st, 16)

        @block.scalar
        def _(act):
            act.wait_ge(c_ld, 16)
            act.activation(cond[:, 1, :], cond[:, 0, :], ACT.Silu).then_inc(cond_ready, 1)

        @block.tensor
        def _(pe):
            pe.sem_inc(mm[0], 1)
            pe.sem_inc(mm[1], 1)
            pe.wait_ge(cond_ready, 1)
            with pe.Fori(0, chunks) as n:
                for l in range(2):
                    pe.wait_ge(w_ld[l], 16 * n + 16)
                    pe.wait_ge(free[l], n + 1)
                    for k in range(KD):
                        last = pe.matmul(ps[l][0:1, :], cond[:, 1, k:k + 1], w[l][:, k, :],
                                         start=k == 0, stop=k == KD - 1)
                    last.then_inc(mm[l], 1)

        @block.vector
        def _(dve):
            dve.sem_inc(free[0], 1)
            dve.sem_inc(free[1], 1)
            dve.wait_ge(b_ld, 16)
            with dve.Fori(0, chunks) as n:
                for l in range(2):
                    dve.wait_ge(mm[l], n + 2)
                    dve.tensor_tensor(mod[:, l, bass.ts(n, HALF)], ps[l][0:1, :],
                                      bias[:, l, bass.ts(n, HALF)], ALU.add).then_inc(free[l], 1)
                    dve.wait_ge(free[l], n + 2)
                    dve.sem_inc(done, 1)



def load_mod(sp, mod_dram, layer, which, dst, sem):
    sp.dma_start(dst, row(mod_dram[layer:layer + 1, :], which * D, D)).then_inc(sem, 16)


def fold_scale(dve, chain, gain, scale):
    chain(dve.scalar_tensor_tensor(out=gain, in0=scale, scalar=1.0, in1=gain, op0=ALU.add, op1=ALU.mult))



def ssm_input(core, ident, x, norm_g, w_in, mod_dram, u_dram):
    nc = core.nc
    BLK = 8
    x_view = x.rearrange("b (c t) d -> t c (b d)", t=L)
    u_view = u_dram.rearrange("g c (n f) -> n c g f", f=BLK * CH)
    const_ld, w_ld, x_ld = core.sem("a_const_loaded"), core.sem("a_w_loaded"), core.sem("a_x_loaded", 2)
    w_hi_ready, w_ready = core.sem("a_w_hi_ready"), core.sem("a_w_split")
    step, var, std = core.sem("a_dve_step"), core.sem("a_var_ready", 2), core.sem("a_std_ready", 2)
    hn_ready = core.sem("a_hn_ready", 2)
    tp, thi, tlo = core.sem("a_transposed", 2), core.sem("a_hT_hi", 2), core.sem("a_hT_lo", 2)
    mm, ev = core.sem("a_product", 2), core.sem("a_evacuated", 2)
    blk_ready, blk_stored = core.sem("a_block_ready"), core.sem("a_block_stored")
    stage_free = core.sem("a_stage_free")
    with ExitStack() as ctx:
        gain, shift = core.sb(ctx, "a_gain", [P, D]), core.sb(ctx, "a_shift", [P, D])
        scale = core.sb(ctx, "a_scale", [P, D])
        w_raw, w_lo = core.raw_low(ctx, "a_w", [P, KD, D])
        w_hi = core.sb(ctx, "a_w_hi", [P, KD, D], F32R)
        xb = core.sbs(ctx, "a_x", 2, [P, D])
        hn = core.sbs(ctx, "a_hn", 2, [P, D])
        stat = core.sbs(ctx, "a_stat", 2, [P, 4])
        h_hi = core.sbs(ctx, "a_hT_hi", 2, [P, KD, P], F32R)
        h_lo = core.sbs(ctx, "a_hT_lo", 2, [P, KD, P], F32R)
        stage = core.sb(ctx, "a_stage", [P, G, BLK * CH])
        pT = [core.ps(ctx, f"a_pT{s}", [P, KD, P]) for s in range(2)]
        pU = [core.ps(ctx, f"a_pU{s}", [P, 2, HALF]) for s in range(2)]
        stage_v = stage[:].rearrange("p g (t f) -> p g t f", f=CH)
        block = ctx.enter_context(nc.Block())

        @block.sync
        def _(sp):
            sp.dma_start(gain[:], row(norm_g[0:1, :], 0, D)).then_inc(const_ld, 16)
            load_mod(sp, mod_dram, 0, SC1, scale[:], const_ld)
            load_mod(sp, mod_dram, 0, SH1, shift[:], const_ld)
            for s in range(2):
                sp.dma_start(xb[s][:], x_view[s]).then_inc(x_ld[s], 16)
            sp.dma_start(w_raw[:], w_in[0].rearrange("(k p) n -> p k n", p=P)).then_inc(w_ld, 16)
            with sp.Fori(1, NT // 2) as i:
                for s in range(2):
                    sp.wait_ge(hn_ready[s], i)
                    sp.dma_start(xb[s][:], x_view[bass.ds(2 * i + s, 1)].squeeze(0)).then_inc(x_ld[s], 16)

        @block.gpsimd
        def _(pool):
            pool.sem_inc(stage_free, 1)
            with pool.Fori(0, NT // BLK) as n:
                pool.wait_ge(blk_ready, BLK * n + BLK)
                pool.dma_start(u_view[bass.ds(n, 1)].squeeze(0), stage[:]).then_inc(blk_stored, 16)
                pool.wait_ge(blk_stored, 16 * n + 16)
                pool.sem_inc(stage_free, 1)

        @block.vector
        def _(dve):
            dve.wait_ge(const_ld, 48)
            chain = Chain(dve, step)
            fold_scale(dve, chain, gain[:], scale[:])
            base = chain.n

            def norm(i, s):
                dve.wait_ge(x_ld[s], 16 * i + 16)
                dve.wait_ge(tp[s], i + 1)
                c = Chain(dve, step, base + 6 * i + 3 * s)
                c(dve.tensor_tensor_reduce(out=hn[s][:], in0=xb[s][:], in1=xb[s][:], scale=1.0, scalar=0.0,
                                           op0=ALU.mult, op1=ALU.add, accum_out=stat[s][:, 0:1]))
                dve.tensor_scalar(stat[s][:, 1:2], stat[s][:, 0:1], 1.0 / D, EPS, ALU.mult, ALU.add) \
                   .then_inc(var[s], 1)
                dve.wait_ge(std[s], i + 1)
                c(dve.reciprocal(stat[s][:, 3:4], stat[s][:, 2:3]))
                c(dve.scalar_tensor_tensor(out=hn[s][:], in0=xb[s][:], scalar=stat[s][:, 3:4], in1=gain[:],
                                           op0=ALU.mult, op1=ALU.mult))
                dve.tensor_tensor(hn[s][:], hn[s][:], shift[:], ALU.add).then_inc(hn_ready[s], 1)

            def low(i, s):
                dve.wait_ge(thi[s], 2 * i + 2)
                dve.tensor_tensor(h_lo[s][:], pT[s][:], h_hi[s][:].bitcast(F32), ALU.subtract) \
                   .then_inc(tlo[s], 1)

            norm(0, 0)
            low(0, 0)
            norm(0, 1)
            for k in range(KD):
                dve.wait_ge(w_hi_ready, k + 1)
                dve.tensor_tensor(w_lo[:, k, :], w_raw[:, k, :], w_hi[:, k, :].bitcast(F32), ALU.subtract) \
                   .then_inc(w_ready, 1)

            def body(i, first, last):
                for s in range(2):
                    if not (last and s == 1):
                        low(*at(i, s, 1))
                    if not last:
                        norm(*at(i, s, 2))
            pairs(dve, NT // 2, body)

        @block.tensor
        def _(pe):
            for s in range(2):
                pe.sem_inc(tp[s], 1)
                pe.sem_inc(mm[s], 2)

            def transposes(i, s):
                pe.wait_ge(hn_ready[s], i + 1)
                pe.wait_ge(tlo[s], i + 1)
                for k in range(KD):
                    last = pe.transpose(pT[s][:, k, :], hn[s][:, k * P:(k + 1) * P], ident[:])
                last.then_inc(tp[s], 1)

            def products(i, s):
                pe.wait_ge(tlo[s], i + 2)
                pe.wait_ge(ev[s], 2 * i + 2)
                for n in range(2):
                    for k in range(KD):
                        last = product(pe, pU[s][:, n, :], (h_hi[s][:, k, :], h_lo[s][:, k, :]),
                                       (w_hi[:, k, bass.ts(n, HALF)], w_lo[:, k, bass.ts(n, HALF)]),
                                       k == 0, k == KD - 1)
                    last.then_inc(mm[s], 1)

            transposes(0, 0)
            pe.wait_ge(w_ready, KD)

            def body(i, first, last):
                for s in range(2):
                    if not (last and s == 1):
                        transposes(*at(i, s, 1))
                    products(i, s)
            pairs(pe, NT // 2, body)

        @block.scalar
        def _(act):
            for s in range(2):
                act.sem_inc(tlo[s], 1)
                act.sem_inc(ev[s], 2)

            def std_of(i, s):
                act.wait_ge(var[s], i + 1)
                act.activation(stat[s][:, 2:3], stat[s][:, 1:2], ACT.Sqrt).then_inc(std[s], 1)

            def high(i, s):
                act.wait_ge(tp[s], i + 2)
                act.wait_ge(mm[s], 2 * i + 2)
                for h in range(2):
                    act.activation(h_hi[s][:, 4 * h:4 * h + 4, :], pT[s][:, 4 * h:4 * h + 4, :], ACT.Copy) \
                       .then_inc(thi[s], 1)

            def evacuate(i, s):
                t = 2 * i + s
                act.wait_ge(stage_free, t // BLK + 1)
                for n in range(2):
                    act.wait_ge(mm[s], 2 * i + n + 3)
                    act.activation(stage_v[:, n * 32:n * 32 + 32, bass.ds(t % BLK, 1), :].squeeze(2),
                                   pU[s][:, n, :].rearrange("p (g f) -> p g f", f=CH), ACT.Copy) \
                       .then_inc(ev[s], 1)
                act.wait_ge(ev[s], 2 * i + 4)
                act.sem_inc(blk_ready, 1)

            std_of(0, 0)
            high(0, 0)
            std_of(0, 1)
            act.wait_ge(w_ld, 16)
            for k in range(KD):
                act.activation(w_hi[:, k, :], w_raw[:, k, :], ACT.Copy).then_inc(w_hi_ready, 1)

            def body(i, first, last):
                for s in range(2):
                    if not (last and s == 1):
                        high(*at(i, s, 1))
                    if not last:
                        std_of(*at(i, s, 2))
                    evacuate(i, s)
            pairs(act, NT // 2, body)


def ssm_tables(core, ident, lam_re, lam_im, log_dt, b_re, b_im, c_re, c_im, d_skip, tab):
    nc = core.nc
    TWO_PI = 2 * np.pi
    C1 = 6.28125
    C2 = float(np.float32(TWO_PI - C1))
    ld = core.sem("t_loaded")
    step, pre, tp, done = core.sem("t_dve_step"), core.sem("t_rows_ready"), core.sem("t_transposed"), core.sem("t_done")
    to_act, to_dve = core.sem("t_for_act"), core.sem("t_from_act")
    sw = core.sem("t_swap_step")
    with ExitStack() as ctx:
        lam = core.sb(ctx, "t_lam", [P, 2, S])
        crow = core.sb(ctx, "t_crow", [P, 2, 8, 2, S])
        lt = core.sb(ctx, "t_lamT", [P, 2, G])
        dt_b = core.sb(ctx, "t_dt", [P, G])
        X, Y = core.sb(ctx, "t_bx", [P, G, CH]), core.sb(ctx, "t_by", [P, G, CH])
        tmp, tmp2 = core.sb(ctx, "t_tmp", [P, G, CH]), core.sb(ctx, "t_tmp2", [P, G, CH])
        ab = core.sb(ctx, "t_ab", [P, 14, G])
        ki = core.sb(ctx, "t_turns", [P, G], I32)
        sg = core.sb(ctx, "t_sign", [P, 1])
        ps_l = core.ps(ctx, "t_pl", [P, 2, G])
        ps_c = [core.ps(ctx, f"t_pc{n}", [P, 8, P]) for n in range(2)]
        block = ctx.enter_context(nc.Block())
        lr, li = lt[:, 0, :], lt[:, 1, :]

        @block.sync
        def _(sp):
            n = 0
            def get(dst, src, slow=False):
                sp.dma_start(dst, src, allow_slow_non_contiguous=slow).then_inc(ld, 16)
            for h in range(2):
                get(lam[0:S, h, :], lam_re[0])
                get(lam[S:P, h, :], lam_im[0])
                hs = slice(h * S, h * S + S)
                get(X[hs], (b_re, b_im)[h][0].rearrange("g p c -> p g c"))
                get(Y[hs], (b_im, b_re)[h][0].rearrange("g p c -> p g c"))
                for n, src in enumerate(((c_re, c_im), (c_im, c_re))):
                    get(crow[:, n, :, h, :], src[h][0].rearrange("(a g) c p -> (g c) a p", g=8))
            get(dt_b[:], log_dt.broadcast_to([P, G]))
            for i in range(SB):
                get(tab.skip[i * CH:(i + 1) * CH, :], d_skip[0].rearrange("(g c) -> c g", c=CH), True)

        loads = 16 * (12 + 1 + SB)

        @block.gpsimd
        def _(pool):
            c = Chain(pool, sw)
            c(pool.memset(tab.swap[:], 0.0))
            for off in (-S, S):
                c(pool.affine_select(out=tab.swap[:], in_=tab.swap[:], compare_op=ALU.not_equal, fill=1.0,
                                     base=off, pattern=[[-1, P]], channel_multiplier=1))

        @block.tensor
        def _(pe):
            pe.wait_ge(ld, loads)
            pe.transpose(ps_l[:].rearrange("p a g -> p (a g)"), lam[:].rearrange("p a s -> p (a s)"), ident[:])
            pe.wait_ge(pre, 1)
            for n in range(2):
                for a in range(8):
                    last = pe.transpose(ps_c[n][:, a, :], crow[:, n, a, :, :].rearrange("p h s -> p (h s)"), ident[:])
            last.then_inc(tp, 1)

        @block.scalar
        def _(act):
            act.wait_ge(to_act, 1)
            act.activation(ab[:, 0, :], dt_b[:], ACT.Exp).then_inc(to_dve, 1)
            act.wait_ge(to_act, 2)
            act.activation(ab[:, 2, :], ab[:, 1, :], ACT.Exp).then_inc(to_dve, 1)
            act.wait_ge(to_act, 3)
            act.activation(ab[:, 4, :], ab[:, 3, :], ACT.Sin)
            act.activation(ab[:, 5, :], ab[:, 3, :], ACT.Sin, scale=0.5).then_inc(to_dve, 1)

        @block.vector
        def _(dve):
            c = Chain(dve, step)
            tt, ts, stt = dve.tensor_tensor, dve.tensor_scalar, dve.scalar_tensor_tensor
            dve.wait_ge(ld, loads)
            c(ts(crow[:, 0, :, 1, :], crow[:, 0, :, 1, :], -1.0, None, ALU.mult))
            c(ts(crow[:, 1, :, :, :], crow[:, 1, :, :, :], -1.0, None, ALU.mult))
            dve.sem_inc(pre, 1)
            dve.sem_inc(to_act, 1)
            c(dve.memset(sg[0:S, :], -1.0))
            c(dve.memset(sg[S:P, :], 1.0))
            dve.wait_ge(tp, 1)
            c(dve.tensor_copy(lt[:], ps_l[:]))
            for n, dst in enumerate((tab.c1, tab.c2)):
                c(dve.tensor_copy(dst[:], ps_c[n][:].rearrange("p a (g c) -> p (a g) c", c=CH)))
            dve.wait_ge(to_dve, 1)
            c(tt(ab[:, 1, :], lr, ab[:, 0, :], ALU.mult))
            dve.sem_inc(to_act, 1)
            c(tt(ab[:, 6, :], li, ab[:, 0, :], ALU.mult))
            c(ts(ab[:, 7, :], ab[:, 6, :], 1 / TWO_PI, None, ALU.mult))
            c(dve.tensor_copy(ki[:], ab[:, 7, :]))
            c(dve.tensor_copy(ab[:, 7, :], ki[:]))
            c(stt(out=ab[:, 6, :], in0=ab[:, 7, :], scalar=-C1, in1=ab[:, 6, :], op0=ALU.mult, op1=ALU.add))
            c(stt(out=ab[:, 6, :], in0=ab[:, 7, :], scalar=-C2, in1=ab[:, 6, :], op0=ALU.mult, op1=ALU.add))
            for cmp, turn in ((ALU.is_gt, -TWO_PI), (ALU.is_lt, TWO_PI)):
                c(ts(ab[:, 7, :], ab[:, 6, :], float(np.float32(np.pi)) * (1 if cmp == ALU.is_gt else -1), turn,
                     cmp, ALU.mult))
                c(tt(ab[:, 6, :], ab[:, 6, :], ab[:, 7, :], ALU.add))
            c(ts(ab[:, 3, :], ab[:, 6, :], 3.1415925, -3.1415925, ALU.min, ALU.max))
            dve.sem_inc(to_act, 1)
            dve.wait_ge(to_dve, 3)
            c(tt(ab[:, 6, :], ab[:, 5, :], ab[:, 5, :], ALU.mult))
            c(ts(ab[:, 6, :], ab[:, 6, :], -2.0, 1.0, ALU.mult, ALU.add))
            c(dve.memset(tab.pr[:, :, 0:1], 1.0))
            c(dve.memset(tab.pi[:, :, 0:1], 0.0))
            ar, ai = tab.pr[:, :, 1], tab.pi[:, :, 1]
            c(tt(ar, ab[:, 2, :], ab[:, 6, :], ALU.mult))
            c(tt(ai, ab[:, 2, :], ab[:, 4, :], ALU.mult))
            c(tt(ab[:, 7, :], lr, lr, ALU.mult))
            c(tt(ab[:, 8, :], li, li, ALU.mult))
            c(tt(ab[:, 7, :], ab[:, 7, :], ab[:, 8, :], ALU.add))
            c(dve.reciprocal(ab[:, 8, :], ab[:, 7, :]))
            c(ts(ab[:, 9, :], ar, -1.0, None, ALU.add))
            c(tt(ab[:, 10, :], ab[:, 9, :], lr, ALU.mult))
            c(tt(ab[:, 11, :], ai, li, ALU.mult))
            c(tt(ab[:, 10, :], ab[:, 10, :], ab[:, 11, :], ALU.add))
            c(tt(ab[:, 10, :], ab[:, 10, :], ab[:, 8, :], ALU.mult))
            c(tt(ab[:, 11, :], ai, lr, ALU.mult))
            c(tt(ab[:, 12, :], ab[:, 9, :], li, ALU.mult))
            c(tt(ab[:, 11, :], ab[:, 11, :], ab[:, 12, :], ALU.subtract))
            c(tt(ab[:, 11, :], ab[:, 11, :], ab[:, 8, :], ALU.mult))
            wide = lambda a: a.unsqueeze(2).broadcast_to([P, G, CH])
            cfr, cfi = wide(ab[:, 10, :]), wide(ab[:, 11, :])
            c(tt(tab.b1[:], X[:], cfr, ALU.mult))
            c(tt(tmp[:], Y[:], cfi, ALU.mult))
            c(stt(out=tab.b1[:], in0=tmp[:], scalar=sg[:, 0:1], in1=tab.b1[:], op0=ALU.mult, op1=ALU.add))
            c(tt(tmp[:], X[:], cfi, ALU.mult))
            c(tt(tmp2[:], Y[:], cfr, ALU.mult))
            c(stt(out=tab.b2[:], in0=tmp2[:], scalar=sg[:, 0:1], in1=tmp[:], op0=ALU.mult, op1=ALU.subtract))
            m = 1
            q1, q2 = tmp, tmp2
            while m < L:
                sr, si = tab.pr[:, :, 1:m + 1], tab.pi[:, :, 1:m + 1]
                mr = tab.pr[:, :, m:m + 1].broadcast_to([P, G, m])
                mi = tab.pi[:, :, m:m + 1].broadcast_to([P, G, m])
                dr, di = tab.pr[:, :, m + 1:2 * m + 1], tab.pi[:, :, m + 1:2 * m + 1]
                a, b = q1[:, :, 0:m], q2[:, :, 0:m]
                c(tt(dr, sr, mr, ALU.mult))
                c(tt(a, si, mi, ALU.mult))
                c(tt(di, sr, mi, ALU.mult))
                c(tt(b, si, mr, ALU.mult))
                c(tt(dr, dr, a, ALU.subtract))
                c(tt(di, di, b, ALU.add))
                m *= 2
            c(dve.tensor_copy(tab.back_r[:], tab.pr[:, :, L - 1::-1]))
            c(dve.tensor_copy(tab.back_i[:], tab.pi[:, :, L - 1::-1]))
            hr, hi = tab.ha, tab.hb
            c(dve.tensor_copy(hr[:, :, 0], tab.pr[:, :, L]))
            c(dve.tensor_copy(hi[:, :, 0], tab.pi[:, :, L]))
            for k in range(1, LEVELS):
                c(tt(ab[:, 0, :], hi[:, :, k - 1], hi[:, :, k - 1], ALU.mult))
                c(tt(hr[:, :, k], hr[:, :, k - 1], hr[:, :, k - 1], ALU.mult))
                c(tt(hr[:, :, k], hr[:, :, k], ab[:, 0, :], ALU.subtract))
                c(stt(out=hi[:, :, k], in0=hr[:, :, k - 1], scalar=2.0, in1=hi[:, :, k - 1],
                      op0=ALU.mult, op1=ALU.mult))
            c(ts(hi[:], hi[:], sg[:, 0:1], -1.0, ALU.mult, ALU.mult))


def ssm_scan(core, ident, tab, u_dram, y_dram):
    nc = core.nc
    BG = 4
    NB = G // BG
    y_view = y_dram.rearrange("(c t) (n f) -> n c t f", t=L, f=2 * BG * CH)
    u_ld, pool_terms, terms_used = core.sem("s_u_loaded", 2), core.sem("s_pool_terms", 2), core.sem("s_terms_used", 2)
    tabs, zeroed = core.sem("s_tables", 2), core.sem("s_zeroed")
    ut_psum, ut_out = core.sem("s_uT_in_psum"), core.sem("s_uT_out")
    p_psum, p_out = core.sem("s_p_in_psum"), core.sem("s_p_out")
    r_psum, r_out = core.sem("s_r_in_psum"), core.sem("s_r_out")
    v_psum, diags, mats = core.sem("s_v_in_psum"), core.sem("s_diagonals"), core.sem("s_scan_matrices")
    copied, level = core.sem("s_scan_copied"), core.sem("s_scan_level")
    y_psum, y_out, y_st, stage_free = core.sem("s_y_in_psum"), core.sem("s_y_out"), core.sem("s_y_stored"), core.sem("s_stage_free")
    batch_done = core.sem("s_batch_done")
    vstep = core.sem("s_dve_step")
    with ExitStack() as ctx:
        us = core.sbs(ctx, "s_u", 2, [P, KB, P])
        t2o, t2p = core.sbs(ctx, "s_t2o", 2, [P, L + 1, CH]), core.sbs(ctx, "s_t2p", 2, [P, L, CH])
        pt = core.sbs(ctx, "s_pt", 2, [P, L, CH])
        z = core.sbs(ctx, "s_z", 2, [P, 2 * SB - 1, CH])
        pw = core.sbs(ctx, "s_p", 2, [P, KB, P])
        uT = [core.sbs(ctx, f"s_uT{b}_", BG, [P, KB, P]) for b in range(2)]
        O = [core.sbs(ctx, f"s_o{b}_", BG, [P, L + 1, CH]) for b in range(2)]
        R = [core.sbs(ctx, f"s_r{b}_", BG, [P, L, CH]) for b in range(2)]
        M = core.sbs(ctx, "s_m", 2, [P, BG, LEVELS, P])
        sc = core.sb(ctx, "s_copy", [P, BG, P])
        sx = core.sb(ctx, "s_before", [P, BG, P])
        stage = core.sb(ctx, "s_stage", [P, L, 2 * BG * CH])
        pU, pP, pR = core.ps(ctx, "s_pU", [P, KB, P]), core.ps(ctx, "s_pP", [P, KB, P]), core.ps(ctx, "s_pR", [P, L, CH])
        pV = [core.ps(ctx, f"s_pV{b}", [P, BG, P]) for b in range(2)]
        pY = [core.ps(ctx, f"s_pY{b}", [P, L, CH]) for b in range(2)]
        flat = lambda a: a.rearrange("p a b -> p (a b)")
        block = ctx.enter_context(nc.Block())

        def number(i, s, g):
            return (2 * i + s) * BG + g

        def turn(i, s, g):
            return (2 * i + s) * (BG // 2) + g // 2

        @block.sync
        def _(sp):
            sp.sem_inc(stage_free, 1)

            def load(i, s):
                for g in range(BG):
                    n = number(i, s, g)
                    sp.wait_ge(ut_psum, n + 1)
                    sp.dma_start(flat(us[g % 2][:]), u_dram[bass.ds(n, 1)].squeeze(0)).then_inc(u_ld[g % 2], 16)

            def store(i):
                sp.wait_ge(y_out, 2 * BG * i + 2 * BG + 2)
                sp.dma_start(y_view[bass.ds(i, 1)].squeeze(0), stage[:]).then_inc(y_st, 16)
                sp.wait_ge(y_st, 16 * i + 16)
                sp.sem_inc(stage_free, 1)

            load(0, 0)
            load(0, 1)
            with sp.Fori(0, NB // 2 - 1) as i:
                load(i + 1, 0)
                store(i)
                load(i + 1, 1)
            store(NB // 2 - 1)

        @block.gpsimd
        def _(pool):
            for q in range(2):
                pool.memset(z[q][:], 0.0).then_inc(zeroed, 1)
            with pool.Fori(0, NB // 2) as i:
                for s in range(2):
                    for g in range(BG):
                        q, gs, r = g % 2, bass.ds(number(i, s, g), 1), turn(i, s, g)
                        ai = tab.pi[:, gs, :].squeeze(1)
                        pool.wait_ge(terms_used[q], r + 1)
                        pool.tensor_tensor(t2o[q][:], tab.c2[:, gs, :].broadcast_to([P, L + 1, CH]),
                                           ai.unsqueeze(2).broadcast_to([P, L + 1, CH]), ALU.mult) \
                            .then_inc(pool_terms[q], 1)
                        pool.tensor_tensor(t2p[q][:], tab.b2[:, gs, :].broadcast_to([P, L, CH]),
                                           tab.back_i[:, gs, :].squeeze(1).unsqueeze(2).broadcast_to([P, L, CH]), ALU.mult) \
                            .then_inc(pool_terms[q], 1)

        @block.vector
        def _(dve):
            for q in range(2):
                dve.sem_inc(terms_used[q], 1)
            dve.sem_inc(p_out, 1)
            dve.sem_inc(r_out, 1)
            dve.wait_ge(zeroed, 2)
            Chain(dve, vstep)(dve.memset(sx[:, :, 0:1], 0.0))

            def tables(i, s, g):
                q, n, r = g % 2, number(i, s, g), turn(i, s, g)
                gs = bass.ds(n, 1)
                ar, ar_back = tab.pr[:, gs, :].squeeze(1), tab.back_r[:, gs, :].squeeze(1)
                c = Chain(dve, vstep, 1 + 5 * n)
                c(dve.tensor_tensor(O[s][g][:], tab.c1[:, gs, :].broadcast_to([P, L + 1, CH]),
                                    ar.unsqueeze(2).broadcast_to([P, L + 1, CH]), ALU.mult))
                c(dve.tensor_tensor(pt[q][:], tab.b1[:, gs, :].broadcast_to([P, L, CH]),
                                    ar_back.unsqueeze(2).broadcast_to([P, L, CH]), ALU.mult))
                c(dve.tensor_single_scalar(z[q][:, SB - 1, :], tab.b1[:, gs, :].squeeze(1), 1.0, ALU.mult))
                dve.wait_ge(pool_terms[q], 2 * r + 2)
                c(dve.tensor_tensor(O[s][g][:], O[s][g][:], t2o[q][:], ALU.add))
                c(dve.tensor_tensor(pt[q][:], pt[q][:], t2p[q][:], ALU.add))
                dve.sem_inc(terms_used[q], 1)
                dve.sem_inc(tabs[q], 1)

            def out_p(i, s, g):
                dve.wait_ge(p_psum, number(i, s, g) + 1)
                dve.tensor_copy(pw[g % 2][:], pP[:]).then_inc(p_out, 1)

            def out_r(i, s, g):
                n = number(i, s, g)
                dve.wait_ge(r_psum, n + 1)
                r = flat(R[s][g][:])
                dve.scalar_tensor_tensor(out=r[:, 0:P], in0=ident[:], scalar=tab.skip[:, bass.ds(n, 1)],
                                         in1=flat(pR[:])[:, 0:P], op0=ALU.mult, op1=ALU.add)
                dve.tensor_copy(r[:, P:], flat(pR[:])[:, P:]).then_inc(r_out, 1)

            def matrices(i, s, g):
                n = number(i, s, g)
                dve.wait_ge(diags, LEVELS * n + LEVELS)
                for k in range(LEVELS):
                    m = M[s][:, g, k, :]
                    last = dve.scalar_tensor_tensor(out=m, in0=tab.swap[:], scalar=tab.hb[:, bass.ds(n, 1), k],
                                                    in1=m, op0=ALU.mult, op1=ALU.add)
                last.then_inc(mats, 1)

            def prepare(i, s):
                for g in range(BG + 1):
                    if g < BG:
                        tables(i, s, g)
                        out_p(i, s, g)
                    if g > 0:
                        out_r(i, s, g - 1)
                        matrices(i, s, g - 1)

            prepare(0, 0)

            def body(i, first, last):
                for s in range(2):
                    if not (last and s == 1):
                        ii, ss = at(i, s, 1)
                        dve.wait_ge(batch_done, 2 * ii + ss)
                        prepare(ii, ss)
            pairs(dve, NB // 2, body)

        @block.scalar
        def _(act):
            act.sem_inc(ut_out, 1)
            act.sem_inc(y_out, 2)

            def prepare(i, s, g):
                n = number(i, s, g)
                act.wait_ge(ut_psum, n + 3)
                act.activation(uT[s][g][:], pU[:], ACT.Copy).then_inc(ut_out, 1)
                for k in range(LEVELS):
                    act.activation(M[s][:, g, k, :], ident[:], ACT.Copy, scale=tab.ha[:, bass.ds(n, 1), k]) \
                       .then_inc(diags, 1)

            def copy(i, s, k):
                b = 2 * i + s
                if k == 0:
                    act.wait_ge(v_psum, b + 1)
                    act.wait_ge(level, LEVELS * b + 1)
                else:
                    act.wait_ge(level, LEVELS * b + k + 1)
                act.activation(sc[:], pV[s][:], ACT.Copy).then_inc(copied, 1)

            def before(i, s):
                b = 2 * i + s
                act.wait_ge(level, LEVELS * b + LEVELS + 1)
                act.wait_ge(batch_done, b + 1)
                act.activation(sx[:, :, 1:P], pV[s][:, :, 0:P - 1], ACT.Copy).then_inc(copied, 1)

            def gelu(i, s):
                if s == 0:
                    act.wait_ge(stage_free, i + 1)
                for g in range(BG):
                    act.wait_ge(y_psum, number(i, s, g) + 1)
                    q = (s * BG + g) * CH
                    act.activation(stage[:, :, q:q + CH], pY[g % 2][:], ACT.Gelu_apprx_tanh).then_inc(y_out, 1)

            for g in range(BG):
                prepare(0, 0, g)

            def body(i, first, last):
                for s in range(2):
                    if not (last and s == 1):
                        ii, ss = at(i, s, 1)
                        act.wait_ge(batch_done, 2 * ii + ss)
                    for k in range(LEVELS):
                        copy(i, s, k)
                        if k < BG and not (last and s == 1):
                            prepare(ii, ss, k)
                    before(i, s)
                    gelu(i, s)
            pairs(act, NB // 2, body)

        @block.tensor
        def _(pe):
            pe.sem_inc(ut_psum, 2)
            pe.sem_inc(batch_done, 1)
            pe.sem_inc(level, 1)

            def turned(i, s, g):
                n, q, r = number(i, s, g), g % 2, turn(i, s, g)
                pe.wait_ge(u_ld[q], 16 * r + 16)
                pe.wait_ge(ut_out, n + 1)
                for k in range(KB):
                    last = pe.transpose(pU[:, k, :], us[q][:, k, :], ident[:])
                last.then_inc(ut_psum, 1)
                pe.wait_ge(tabs[q], r + 1)
                pe.wait_ge(p_out, n + 1)
                for k in range(KB):
                    last = pe.transpose(pP[:, k, :], flat(pt[q][:])[:, k * P:(k + 1) * P], ident[:])
                last.then_inc(p_psum, 1)

            def inner(i, s, g):
                n, q = number(i, s, g), g % 2
                pe.wait_ge(ut_out, n + 2)
                pe.wait_ge(p_out, n + 2)
                for k in range(KB):
                    last = pe.matmul(pV[s][:, g, :], pw[q][:, k, :], uT[s][g][:, k, :],
                                     start=(g == 0 and k == 0), stop=False, skip_group_check=True)
                if g == BG - 1:
                    last.then_inc(v_psum, 1)
                pe.wait_ge(r_out, n + 1)
                o, r = flat(O[s][g][:]), flat(pR[:])
                for j in range(SB):
                    pe.matmul(r[:, j * CH:P], flat(z[q][:])[:, (SB - 1 - j) * CH:(SB - 1 - j) * CH + P],
                              o[:, 0:(SB - j) * CH], start=j == 0, stop=False, skip_group_check=True)
                pe.matmul(r[:, P:], flat(pt[q][:])[:, (KB - 1) * P:], o[:, CH:CH + (KB - 1) * P],
                          start=False, stop=True, skip_group_check=True).then_inc(r_psum, 1)

            def scan(i, s, k):
                b = 2 * i + s
                if k == 0:
                    pe.wait_ge(mats, BG * b + BG)
                pe.wait_ge(copied, (LEVELS + 1) * b + k + 1)
                h = 1 << k
                for g in range(BG):
                    last = pe.matmul(pV[s][:, g, h:], M[s][:, g, k, :], sc[:, g, 0:P - h], start=False,
                                     stop=(k == LEVELS - 1 and g == BG - 1), skip_group_check=True)
                last.then_inc(level, 1)

            def answer(i, s):
                b = 2 * i + s
                pe.wait_ge(copied, (LEVELS + 1) * (b + 1))
                for g in range(BG):
                    n = number(i, s, g)
                    pe.wait_ge(y_out, n + 1)
                    pe.wait_ge(r_out, n + 2)
                    y, r, o = flat(pY[g % 2][:]), flat(R[s][g][:]), flat(O[s][g][:])
                    for k in range(KB):
                        pe.matmul(y[:, k * P:], uT[s][g][:, k, :], r[:, 0:(KB - k) * P],
                                  start=k == 0, stop=False, skip_group_check=True)
                    last = pe.matmul(y, sx[:, g, :], o[:, CH:], start=False, stop=True, skip_group_check=True)
                    last.then_inc(y_psum, 1)
                pe.wait_ge(y_psum, BG * b + BG)
                pe.sem_inc(batch_done, 1)

            for g in range(BG + 1):
                if g < BG:
                    turned(0, 0, g)
                if g > 0:
                    inner(0, 0, g - 1)

            def body(i, first, last):
                for s in range(2):
                    more = not (last and s == 1)
                    ii, ss = at(i, s, 1)
                    for k in range(LEVELS):
                        scan(i, s, k)
                        if more and k < BG:
                            turned(ii, ss, k)
                        if more and 0 < k <= BG:
                            inner(ii, ss, k - 1)
                    answer(i, s)
            pairs(pe, NB // 2, body)


class SsmTables:

    def __init__(self, core, ctx):
        self.pr, self.pi = core.sbs(ctx, "pow", 2, [P, G, L + 1])
        self.back_r, self.back_i = core.sbs(ctx, "pow_back", 2, [P, G, L])
        self.ha, self.hb = core.sbs(ctx, "pow_high", 2, [P, G, LEVELS])
        self.b1, self.b2, self.c1, self.c2 = core.sbs(ctx, "bc", 4, [P, G, CH])
        self.skip = core.sb(ctx, "skip", [P, G])
        self.swap = core.sb(ctx, "swap", [P, P])



NL = NG + NE


def project(core, ident, tag, layer, glu, src, w, x_view, norm_g, wg, bg, we, be, mod_dram, x1_dram, hn_dram, logits):
    nc = core.nc
    sem = lambda name, n=None: core.sem(f"{tag}_{name}", n)
    NB_ = (4 if glu else 2)
    const_ld, w_ld, s_ld, x_ld = sem("const_loaded"), sem("w_loaded", KD), sem("src_loaded", 2), sem("x_loaded", 2)
    w_hi_ready, w_split, step = sem("w_hi"), sem("w_split"), sem("dve_step")
    tp, thi, tlo, mm = sem("transposed", 2), sem("hi", 2), sem("lo", 2), sem("bank")
    gated, out_read = sem("gate"), sem("product_read")
    x1_ready, x1_st, hn_st = sem("x1_ready", 2), sem("x1_stored", 2), sem("hn_stored", 2)
    var, std, hn_ready = sem("var"), sem("std"), sem("hn_ready", 2)
    ht_psum, ht_out, lg_psum, lg_out = sem("hT_in_psum"), sem("hT_out"), sem("logits_in_psum"), sem("logits_out")
    with ExitStack() as ctx:
        sb = lambda name, shape, dt=F32: core.sb(ctx, f"{tag}_{name}", shape, dt)
        sbs = lambda name, n, shape, dt=F32: core.sbs(ctx, f"{tag}_{name}", n, shape, dt)
        cols = NB_ * HALF
        w_raw, w_lo = core.raw_low(ctx, f"{tag}_w", [P, KD, cols])
        w_hi = sb("w_hi", [P, KD, cols], F32R)
        gate1, gain, shift = sb("gate1", [P, D]), sb("gain", [P, D]), sb("shift", [P, D])
        wr, br = sb("router", [P, KD, NL]), sb("router_bias", [P, NL])
        srcb = sbs("src", 2, [P, KD, P])
        xb, hn = sbs("x", 2, [P, D]), sbs("hn", 2, [P, D])
        h_hi, h_lo = sbs("sT_hi", 2, [P, KD, P], F32R), sbs("sT_lo", 2, [P, KD, P], F32R)
        acc = sb("acc", [P, 2, HALF])
        hT = sb("hT", [P, KD, P])
        stat = sbs("stat", 2, [P, 4])
        pT = core.ps(ctx, f"{tag}_pT", [P, KD, P]) if glu else None
        pM = core.ps(ctx, f"{tag}_pM", [P, NB_, HALF])
        pH = core.ps(ctx, f"{tag}_pH", [P, KD, P])
        accf = acc[:].rearrange("p a b -> p (a b)")
        block = ctx.enter_context(nc.Block())
        order = (2, 3, 0, 1) if glu else (0, 1)
        if glu:
            src_view = src.rearrange("(n p) (k f) -> n p k f", p=P, f=P)
        else:
            src_view = src.rearrange("(k p) (n f) -> n p k f", p=P, f=P)
        x1_view = x1_dram.rearrange("(n p) d -> n p d", p=P)
        hn_view = hn_dram.rearrange("(n p) d -> n p d", p=P)
        tile_of = lambda view, i, s: view[bass.ds(2 * i + s, 1)].squeeze(0)

        @block.sync
        def _(sp):
            def load_src(i, s):
                sp.wait_ge(tlo[s], i + 1)
                sp.dma_start(srcb[s][:], tile_of(src_view, i, s)).then_inc(s_ld[s], 16)

            def load_x(i, s):
                sp.dma_start(xb[s][:], tile_of(x_view, i, s)).then_inc(x_ld[s], 16)

            def store(i, s):
                sp.wait_ge(x1_ready[s], i + 1)
                sp.dma_start(tile_of(x1_view, i, s), xb[s][:]).then_inc(x1_st[s], 16)
                sp.wait_ge(hn_ready[s], i + 1)
                sp.dma_start(tile_of(hn_view, i, s), hn[s][:]).then_inc(hn_st[s], 16)

            sp.dma_start(gate1[:], row(mod_dram[layer:layer + 1, :], G1 * D, D)).then_inc(const_ld, 16)
            sp.dma_start(gain[:], row(norm_g[layer:layer + 1, :], 0, D)).then_inc(const_ld, 16)
            load_mod(sp, mod_dram, layer, SC2, hn[0][:], const_ld)
            load_mod(sp, mod_dram, layer, SH2, shift[:], const_ld)
            sp.dma_start(wr[:, :, 0:NG], wg[layer].rearrange("(k p) n -> p k n", p=P)).then_inc(const_ld, 16)
            sp.dma_start(wr[:, :, NG:], we[layer].rearrange("(k p) n -> p k n", p=P)).then_inc(const_ld, 16)
            sp.dma_start(br[:, 0:NG], row(bg[layer:layer + 1, :], 0, NG)).then_inc(const_ld, 16)
            sp.dma_start(br[:, NG:], row(be[layer:layer + 1, :], 0, NE)).then_inc(const_ld, 16)
            load_src(0, 0)
            load_src(0, 1)
            for k in range(KD):
                sp.dma_start(w_raw[:, k, :], w.rearrange("(k p) n -> k p n", p=P)[k]).then_inc(w_ld[k], 16)
            load_x(0, 0)
            load_x(0, 1)
            with sp.Fori(0, NT // 2 - 1) as i:
                for s in range(2):
                    load_src(i + 1, s)
                    store(i, s)
                    sp.wait_ge(x1_st[s], 16 * i + 16)
                    load_x(i + 1, s)
            for s in range(2):
                store(NT // 2 - 1, s)
            for s in range(2):
                sp.wait_ge(x1_st[s], 16 * (NT // 2))
                sp.wait_ge(hn_st[s], 16 * (NT // 2))

        @block.vector
        def _(dve):
            dve.wait_ge(const_ld, 8 * 16)
            base = 2
            c = Chain(dve, step)
            fold_scale(dve, c, gain[:], hn[0][:])
            c(dve.tensor_scalar(gate1[:], gate1[:], 1.0, None, ALU.add))

            def low(i, s):
                dve.wait_ge(thi[s], 2 * i + 2)
                raw = pT if glu else srcb[s]
                dve.tensor_tensor(h_lo[s][:], raw[:], h_hi[s][:].bitcast(F32), ALU.subtract).then_inc(tlo[s], 1)

            def finish(i, s):
                n = 2 * i + s
                c = Chain(dve, step, base + (6 if glu else 5) * n)
                dve.wait_ge(mm, NB_ * n + NB_)
                dve.wait_ge(x_ld[s], 16 * i + 16)
                if glu:
                    dve.wait_ge(gated, 2 * n + 2)
                    c(dve.tensor_tensor(acc[:], pM[:, 0:2, :], acc[:], ALU.mult))
                    dve.sem_inc(out_read, 1)
                    c(dve.tensor_tensor(accf, accf, gate1[:], ALU.mult))
                else:
                    c(dve.tensor_tensor(accf, pM[:].rearrange("p a b -> p (a b)"), gate1[:], ALU.mult))
                    dve.sem_inc(out_read, 1)
                c(dve.tensor_tensor(xb[s][:], accf, xb[s][:], ALU.add))
                dve.sem_inc(x1_ready[s], 1)
                c(dve.tensor_tensor_reduce(out=accf, in0=xb[s][:], in1=xb[s][:], scale=1.0, scalar=0.0,
                                           op0=ALU.mult, op1=ALU.add, accum_out=stat[s][:, 0:1]))
                dve.tensor_scalar(stat[s][:, 1:2], stat[s][:, 0:1], 1.0 / D, EPS, ALU.mult, ALU.add).then_inc(var, 1)
                dve.wait_ge(std, n + 1)
                c(dve.reciprocal(stat[s][:, 3:4], stat[s][:, 2:3]))
                if not (isinstance(i, int) and i == 0):
                    dve.wait_ge(hn_st[s], 16 * i)
                    dve.wait_ge(ht_psum, n)
                c(dve.scalar_tensor_tensor(out=hn[s][:], in0=xb[s][:], scalar=stat[s][:, 3:4], in1=gain[:],
                                           op0=ALU.mult, op1=ALU.mult))
                dve.tensor_tensor(hn[s][:], hn[s][:], shift[:], ALU.add).then_inc(hn_ready[s], 1)

            def out_logits(i, s):
                n = 2 * i + s
                dve.wait_ge(lg_psum, n + 1)
                dve.tensor_tensor(logits[:, bass.ds(n, 1), :].squeeze(1), pH[:, 0, 0:NL], br[:], ALU.add) \
                   .then_inc(lg_out, 1)

            low(0, 0)
            for k in range(KD):
                dve.wait_ge(w_hi_ready, k + 1)
                dve.tensor_tensor(w_lo[:, k, :], w_raw[:, k, :], w_hi[:, k, :].bitcast(F32), ALU.subtract) \
                   .then_inc(w_split, 1)

            def body(i, first, last):
                for s in range(2):
                    if not (last and s == 1):
                        low(*at(i, s, 1))
                    if not first:
                        out_logits(*at(i, s, -2))
                    finish(i, s)
            pairs(dve, NT // 2, body)
            out_logits(NT // 2 - 1, 0)
            out_logits(NT // 2 - 1, 1)

        @block.scalar
        def _(act):
            act.sem_inc(ht_out, 1)
            for s in range(2):
                act.sem_inc(tlo[s], 1)

            def high(i, s):
                if glu:
                    act.wait_ge(tp[s], i + 1)
                else:
                    act.wait_ge(s_ld[s], 16 * i + 16)
                if not (isinstance(i, int) and i == 0):
                    act.wait_ge(mm, NB_ * (2 * i + s) - NB_)
                raw = pT if glu else srcb[s]
                for h in range(2):
                    act.activation(h_hi[s][:, 4 * h:4 * h + 4, :], raw[:, 4 * h:4 * h + 4, :], ACT.Copy) \
                       .then_inc(thi[s], 1)

            def gate(i, s):
                n = 2 * i + s
                act.wait_ge(var, n + 1)
                for h in range(2):
                    act.wait_ge(mm, NB_ * n + h + 1)
                    act.activation(acc[:, h, :], pM[:, 2 + h, :], ACT.Sigmoid).then_inc(gated, 1)

            def std_of(i, s):
                n = 2 * i + s
                act.wait_ge(var, n + (2 if glu else 1))
                act.activation(stat[s][:, 2:3], stat[s][:, 1:2], ACT.Sqrt).then_inc(std, 1)

            def out_h(i, s):
                n = 2 * i + s
                act.wait_ge(ht_psum, n + 2)
                act.activation(hT[:], pH[:], ACT.Copy).then_inc(ht_out, 1)

            if glu:
                act.sem_inc(var, 1)
            high(0, 0)
            for k in range(KD):
                act.wait_ge(w_ld[k], 16)
                act.activation(w_hi[:, k, :], w_raw[:, k, :], ACT.Copy).then_inc(w_hi_ready, 1)

            def body(i, first, last):
                for s in range(2):
                    if not (last and s == 1):
                        high(*at(i, s, 1))
                    if glu:
                        gate(i, s)
                    if not (first and s == 0):
                        out_h(*at(i, s, -1))
                    std_of(i, s)
            pairs(act, NT // 2, body)
            out_h(NT // 2 - 1, 1)

        @block.tensor
        def _(pe):
            pe.sem_inc(ht_psum, 1)
            pe.sem_inc(out_read, 1)

            def turned(i, s):
                pe.wait_ge(s_ld[s], 16 * i + 16)
                pe.wait_ge(tlo[(s + 1) % 2], i + 1 + (0 if s == 0 else 1))
                for k in range(KD):
                    last = pe.transpose(pT[:, k, :], srcb[s][:, k, :], ident[:])
                last.then_inc(tp[s], 1)

            def products(i, s):
                n = 2 * i + s
                pe.wait_ge(tlo[s], i + 2)
                pe.wait_ge(out_read, n + 1)
                for b in order:
                    for k in range(KD):
                        last = product(pe, pM[:, b, :], (h_hi[s][:, k, :], h_lo[s][:, k, :]),
                                       (w_hi[:, k, bass.ts(b, HALF)], w_lo[:, k, bass.ts(b, HALF)]),
                                       k == 0, k == KD - 1)
                    last.then_inc(mm, 1)

            def turned_hn(i, s):
                n = 2 * i + s
                pe.wait_ge(hn_ready[s], i + 1)
                if not (isinstance(n, int) and n == 0):
                    pe.wait_ge(lg_out, n)
                for k in range(KD):
                    last = pe.transpose(pH[:, k, :], hn[s][:, k * P:(k + 1) * P], ident[:])
                last.then_inc(ht_psum, 1)

            def router(i, s):
                n = 2 * i + s
                pe.wait_ge(ht_out, n + 2)
                for k in range(KD):
                    last = pe.matmul(pH[:, 0, 0:NL], hT[:, k, :], wr[:, k, :], start=k == 0, stop=k == KD - 1)
                last.then_inc(lg_psum, 1)

            if glu:
                turned(0, 0)
            pe.wait_ge(w_split, KD)

            def body(i, first, last):
                for s in range(2):
                    if glu and not (last and s == 1):
                        turned(*at(i, s, 1))
                    if not first:
                        router(*at(i, s, -2))
                    products(i, s)
                    if not (first and s == 0):
                        turned_hn(*at(i, s, -1))
            pairs(pe, NT // 2, body)
            router(NT // 2 - 1, 0)
            turned_hn(NT // 2 - 1, 1)
            router(NT // 2 - 1, 1)



def routing(core, tag, logits, pos, wts, experts_row, slot_dram, tile_dram):
    nc = core.nc
    sem = lambda name: core.sem(f"{tag}_{name}")
    step, istep, to_act, to_dve = sem("dve_step"), sem("pool_step"), sem("for_act"), sem("from_act")
    mask_ready, counted, zero_st, pos_ready, sc_st = sem("mask"), sem("counted"), sem("zeroed"), sem("pos_ready"), sem("scattered")
    te_ready, te_st, te_ld = sem("tile_experts"), sem("tile_stored"), sem("tile_loaded")
    with ExitStack() as ctx:
        sb = lambda name, shape, dt=F32: core.sb(ctx, f"{tag}_{name}", shape, dt)
        upper, ones = sb("upper", [P, P]), sb("ones", [P, P])
        io_i, io = sb("iota_i", [P, EG], I32), sb("iota", [P, EG])
        ip_i, ip = sb("iota_p_i", [P, 1], I32), sb("iota_p", [P, 1])
        tok = sb("token", [P, NT], I32)
        zt = sb("zeros", [P, TILES + 1], I32)
        a1, a2, a3 = sb("t1", [P, NT, 1]), sb("t2", [P, NT, 1]), sb("t3", [P, NT, 1])
        m1, m2, gp = sb("m1", [P, NT, 1]), sb("m2", [P, NT, 1]), sb("gp", [P, NT, 1])
        g4, ohg = sb("g4", [P, NT, NG]), sb("ohg", [P, NT, NG])
        es, tmp = sb("e_sel", [P, NT, EG]), sb("tmp", [P, NT, EG])
        ohk = [sb(f"ohk{k}", [P, NT, EG]) for k in range(2)]
        OH = [sb(f"oh{k}", [P, NT, NE]) for k in range(2)]
        M, C0, C1_, V = (sb(n, [P, NT, NE]) for n in ("mask", "c0", "c1", "v"))
        ti, tf, tg = sb("tiles_i", [P, NE], I32), sb("tiles", [P, NE]), sb("tiles2", [P, NE])
        own = sb("own", [P, NE])
        te_f, te_i = sb("te_f", [P, 1]), sb("te_i", [P, 1], I32)
        posf = sb("posf", [P, NT, 2])
        pr = core.ps(ctx, f"{tag}_rank", [P, NT * NE])
        pc = core.ps(ctx, f"{tag}_count", [P, NT * NE])
        block = ctx.enter_context(nc.Block())
        flat = lambda a: a.rearrange("p a b -> p (a b)")

        @block.gpsimd
        def _(pool):
            c = Chain(pool, istep)
            c(pool.memset(ones[:], 1.0))
            c(pool.affine_select(out=upper[:], in_=ones[:], compare_op=ALU.is_gt, fill=0.0, base=0,
                                 pattern=[[1, P]], channel_multiplier=-1))
            c(pool.iota(io_i[:], pattern=[[1, EG]], base=-EG, channel_multiplier=0))
            c(pool.iota(ip_i[:], pattern=[[0, 1]], base=0, channel_multiplier=1))
            c(pool.iota(tok[:], pattern=[[P, NT]], base=0, channel_multiplier=1))
            c(pool.memset(zt[:], 0))
            pool.dma_start(slot_dram.rearrange("(p n) one -> p (n one)", p=P), zt[:]).then_inc(zero_st, 16)
            pool.wait_ge(zero_st, 16)
            pool.wait_ge(pos_ready, 1)
            for t in range(NT):
                for k in range(2):
                    pool.indirect_dma_start(slot_dram, bass.IndirectOffsetOnAxis(ap=pos[:, t, k:k + 1], axis=0),
                                            tok[:, t:t + 1], None).then_inc(sc_st, 16)
            pool.wait_ge(sc_st, 16 * 2 * NT)

        @block.scalar
        def _(act):
            act.wait_ge(to_act, 1)
            act.activation(g4[:], g4[:], ACT.Exp).then_inc(to_dve, 1)
            act.wait_ge(to_act, 2)
            act.activation(a3[:], a3[:], ACT.Exp).then_inc(to_dve, 1)

        @block.tensor
        def _(pe):
            pe.wait_ge(mask_ready, 1)
            for lhs, out in ((upper, pr), (ones, pc)):
                for h in range(2):
                    last = pe.matmul(out[:, h * HALF:(h + 1) * HALF], lhs[:], flat(M[:])[:, h * HALF:(h + 1) * HALF],
                                     start=True, stop=True)
            last.then_inc(counted, 1)

        @block.sync
        def _(sp):
            sp.wait_ge(te_ready, 1)
            sp.dma_start(tile_dram, te_i[:], allow_slow_non_contiguous=True).then_inc(te_st, 16)
            sp.wait_ge(te_st, 16)
            sp.dma_start(experts_row[:], tile_dram.rearrange("n one -> one n")).then_inc(te_ld, 16)
            sp.wait_ge(te_ld, 16)

        @block.vector
        def _(dve):
            c = Chain(dve, step)
            tt, ts, red, copy = dve.tensor_tensor, dve.tensor_scalar, dve.tensor_reduce, dve.tensor_copy
            bc = lambda a, n: a.broadcast_to([P, NT, n])

            def first_of(values, best, n, out):
                t_ = tmp[:, :, 0:n]
                c(tt(t_, values, bc(best, n), ALU.is_equal))
                c(tt(t_, t_, io[:, 0:n].unsqueeze(1).broadcast_to([P, NT, n]), ALU.mult))
                c(red(a2[:], t_, AX.X, ALU.min))
                c(tt(out, io[:, 0:n].unsqueeze(1).broadcast_to([P, NT, n]), bc(a2[:], n), ALU.is_equal))

            dve.wait_ge(istep, 6)
            c(copy(io[:], io_i[:]))
            c(copy(ip[:], ip_i[:]))
            gl = logits[:, :, 0:NG]
            c(red(m1[:], gl, AX.X, ALU.max))
            c(tt(g4[:], gl, bc(m1[:], NG), ALU.subtract))
            dve.sem_inc(to_act, 1)
            first_of(gl, m1[:], NG, ohg[:])
            dve.wait_ge(to_dve, 1)
            c(red(a1[:], g4[:], AX.X, ALU.add))
            c(dve.reciprocal(gp[:], a1[:]))
            for g in range(NG):
                el = logits[:, :, NG + g * EG:NG + (g + 1) * EG]
                dst = es if g == 0 else tmp
                c(tt(dst[:], el, bc(ohg[:, :, g:g + 1], EG), ALU.mult))
                if g:
                    c(tt(es[:], es[:], tmp[:], ALU.add))
            c(red(m1[:], es[:], AX.X, ALU.max))
            first_of(es[:], m1[:], EG, ohk[0][:])
            c(dve.scalar_tensor_tensor(out=es[:], in0=ohk[0][:], scalar=-3.0e38, in1=es[:], op0=ALU.mult, op1=ALU.add))
            c(red(m2[:], es[:], AX.X, ALU.max))
            first_of(es[:], m2[:], EG, ohk[1][:])
            c(tt(a3[:], m2[:], m1[:], ALU.subtract))
            dve.sem_inc(to_act, 1)
            dve.wait_ge(to_dve, 2)
            c(ts(a1[:], a3[:], 1.0, None, ALU.add))
            c(dve.reciprocal(a1[:], a1[:]))
            c(tt(a1[:], a1[:], gp[:], ALU.mult))
            c(copy(wts[:, :, 0:1], a1[:]))
            c(tt(wts[:, :, 1:2], a1[:], a3[:], ALU.mult))
            for k in range(2):
                c(tt(OH[k][:].rearrange("p t (g e) -> p t g e", g=NG),
                     ohg[:].unsqueeze(3).broadcast_to([P, NT, NG, EG]),
                     ohk[k][:].unsqueeze(2).broadcast_to([P, NT, NG, EG]), ALU.mult))
            c(tt(M[:], OH[0][:], OH[1][:], ALU.add))
            dve.sem_inc(mask_ready, 1)
            dve.wait_ge(counted, 1)
            src, dst = C0, C1_
            c(copy(flat(src[:]), pc[:]))
            h = 1
            while h < NT:
                c(copy(dst[:, 0:h, :], src[:, 0:h, :]))
                c(tt(dst[:, h:, :], src[:, h:, :], src[:, 0:NT - h, :], ALU.add))
                src, dst = dst, src
                h *= 2
            c(ts(tf[:], src[:, NT - 1, :], float(P - 1), None, ALU.add))
            c(copy(ti[:], tf[:]))
            c(dve.tensor_single_scalar(ti[:], ti[:], 7, ALU.arith_shift_right))
            c(copy(own[:], ti[:]))
            c(ts(own[:], own[:], 1.0, None, ALU.max))
            c(copy(tf[:], own[:]))
            x, y = tf, tg
            h = 1
            while h < NE:
                c(copy(y[:, 0:h], x[:, 0:h]))
                c(tt(y[:, h:], x[:, h:], x[:, 0:NE - h], ALU.add))
                x, y = y, x
                h *= 2
            c(ts(y[:], x[:], ip[:, 0:1], None, ALU.is_le))
            c(red(te_f[:], y[:], AX.X, ALU.add))
            c(ts(te_f[:], te_f[:], float(NE - 1), None, ALU.min))
            c(copy(te_i[:], te_f[:]))
            dve.sem_inc(te_ready, 1)
            c(tt(x[:], x[:], own[:], ALU.subtract))
            c(ts(x[:], x[:], float(P), None, ALU.mult))
            c(tt(flat(V[:]), flat(src[:]), pc[:], ALU.subtract))
            c(tt(flat(V[:]), flat(V[:]), pr[:], ALU.add))
            c(tt(V[:], V[:], x[:].unsqueeze(1).broadcast_to([P, NT, NE]), ALU.add))
            for k in range(2):
                c(tt(OH[k][:], OH[k][:], V[:], ALU.mult))
                c(red(posf[:, :, k:k + 1], OH[k][:], AX.X, ALU.add))
            c(copy(pos[:], posf[:]))
            dve.sem_inc(pos_ready, 1)



def experts(core, ident, tag, layer, w1, w3, w2, experts_row, slot_dram, hn_dram, o_dram):
    nc = core.nc
    sem = lambda name, n=None: core.sem(f"{tag}_{name}", n)
    w_ld, w_used = sem("w_loaded", 2), sem("w_used", 2)
    ix_ld, x_ld, gath = sem("idx_loaded", 2), sem("rows_loaded", 2), sem("gathers")
    xt_psum, xt_out, ab, hh = sem("xT_in_psum"), sem("xT_out"), sem("ab_in_psum"), sem("h_ready")
    sil, ht_psum, ht_out, o_psum, o_out = sem("silu"), sem("hT_in_psum"), sem("hT_out"), sem("o_in_psum"), sem("o_out")
    o_st = sem("o_stored", 2)
    with ExitStack() as ctx:
        sb = lambda name, shape, dt=F32: core.sb(ctx, f"{tag}_{name}", shape, dt)
        sbs = lambda name, n, shape, dt=F32: core.sbs(ctx, f"{tag}_{name}", n, shape, dt)
        W1, W3, W2 = sbs("w1", 2, [P, KD, FE]), sbs("w3", 2, [P, KD, FE]), sbs("w2", 2, [P, KF, D])
        ix = sbs("idx", 2, [P, 1], I32)
        xg = sbs("rows", 2, [P, D])
        xT = sb("xT", [P, KD, P])
        h = sb("h", [P, FE])
        hT = sb("hT", [P, KF, P])
        ob = sbs("o", 2, [P, 2, HALF])
        pX = core.ps(ctx, f"{tag}_pX", [P, KD, P])
        pA, pB, pH = (core.ps(ctx, f"{tag}_{n}", [P, HALF]) for n in ("pA", "pB", "pH"))
        pO = core.ps(ctx, f"{tag}_pO", [P, 2, HALF])
        block = ctx.enter_context(nc.Block())
        slots = slot_dram.rearrange("(n p) one -> n p one", p=P)
        o_view = o_dram.rearrange("(n p) d -> n p (d)", p=P)
        n_tiles = TILES + 1

        @block.sync
        def _(sp):
            with sp.Fori(0, n_tiles // 2) as i:
                for s in range(2):
                    e = bass.ds(sp.value_load(experts_row[0:1, bass.ds(2 * i + s, 1)], min_val=0, max_val=NE - 1), 1)
                    sp.wait_ge(w_used[s], i + 1)
                    sp.dma_start(W1[s][:], w1[layer, e].squeeze(0).rearrange("(k p) n -> p k n", p=P)).then_inc(w_ld[s], 16)
                    sp.dma_start(W3[s][:], w3[layer, e].squeeze(0).rearrange("(k p) n -> p k n", p=P)).then_inc(w_ld[s], 16)
                    sp.dma_start(W2[s][:], w2[layer, e].squeeze(0).rearrange("(k p) n -> p k n", p=P)).then_inc(w_ld[s], 16)

        @block.gpsimd
        def _(pool):
            with pool.Fori(0, n_tiles // 2) as i:
                for s in range(2):
                    t = 2 * i + s
                    pool.dma_start(ix[s][:], slots[bass.ds(t, 1)].squeeze(0)).then_inc(ix_ld[s], 16)
                    pool.wait_ge(ix_ld[s], 16 * i + 16)
                    pool.wait_ge(xt_psum, t + 1)
                    pool.sem_inc(gath, 1)
                    pool.indirect_dma_start(xg[s][:], None, hn_dram, bass.IndirectOffsetOnAxis(ap=ix[s][:, 0:1], axis=0)) \
                        .then_inc(x_ld[s], 16)
                    pool.wait_ge(x_ld[s], 16 * i + 16)

        @block.tensor
        def _(pe):
            pe.sem_inc(xt_psum, 2)
            for s in range(2):
                pe.sem_inc(w_used[s], 1)

            def turned(i, s):
                t = 2 * i + s
                pe.wait_ge(x_ld[s], 16 * i + 16)
                pe.wait_ge(xt_out, 2 * t + 2)
                for k in range(KD):
                    last = pe.transpose(pX[:, k, :], xg[s][:, k * P:(k + 1) * P], ident[:])
                last.then_inc(xt_psum, 1)

            def tile(i, s, more):
                t = 2 * i + s
                pe.wait_ge(w_ld[s], 48 * i + 48)
                pe.wait_ge(xt_out, 2 * t + 4)
                pe.wait_ge(hh, t + 1)
                for w, out in ((W1, pA), (W3, pB)):
                    for k in range(KD):
                        last = pe.matmul(out[:], xT[:, k, :], w[s][:, k, :], start=k == 0, stop=k == KD - 1)
                    last.then_inc(ab, 1)
                if more:
                    turned(*at(i, s, 1))
                pe.wait_ge(hh, t + 2)
                for k in range(KF):
                    last = pe.transpose(pH[:, k * P:(k + 1) * P], h[:, k * P:(k + 1) * P], ident[:])
                last.then_inc(ht_psum, 1)
                pe.wait_ge(ht_out, t + 1)
                pe.wait_ge(o_out, 2 * t + 2)
                for n in range(2):
                    for k in range(KF):
                        last = pe.matmul(pO[:, n, :], hT[:, k, :], W2[s][:, k, n * HALF:(n + 1) * HALF],
                                         start=k == 0, stop=k == KF - 1)
                    last.then_inc(o_psum, 1)
                pe.wait_ge(o_psum, 2 * t + 2)
                pe.sem_inc(w_used[s], 1)

            turned(0, 0)

            def body(i, first, last):
                for s in range(2):
                    tile(i, s, not (last and s == 1))
            pairs(pe, n_tiles // 2, body)

        @block.scalar
        def _(act):
            act.sem_inc(xt_out, 1)
            act.sem_inc(o_out, 1)

            def out_x(i, s):
                t = 2 * i + s
                act.wait_ge(xt_psum, t + 3)
                act.wait_ge(ab, 2 * t) if not (isinstance(t, int) and t == 0) else None
                act.activation(xT[:, 0:4, :], pX[:, 0:4, :], ACT.Copy).then_inc(xt_out, 1)

            out_x(0, 0)

            def body(i, first, last):
                for s in range(2):
                    t = 2 * i + s
                    act.wait_ge(ab, 2 * t + 1)
                    act.wait_ge(ht_psum, t) if not (isinstance(t, int) and t == 0) else None
                    act.activation(h[:], pA[:], ACT.Silu).then_inc(sil, 1)
                    if not (last and s == 1):
                        out_x(*at(i, s, 1))
                    act.wait_ge(ht_psum, t + 1)
                    act.wait_ge(o_psum, 2 * t) if not (isinstance(t, int) and t == 0) else None
                    act.activation(hT[:].rearrange("p a b -> p (a b)"), pH[:], ACT.Copy).then_inc(ht_out, 1)
                    act.wait_ge(o_psum, 2 * t + 1)
                    act.wait_ge(o_st[s], 16 * i) if not (isinstance(i, int) and i == 0) else None
                    act.activation(ob[s][:, 0, :], pO[:, 0, :], ACT.Copy).then_inc(o_out, 1)
                    act.wait_ge(o_out, 2 * t + 4)
                    act.dma_start(o_view[bass.ds(t, 1)].squeeze(0), ob[s][:].rearrange("p a b -> p (a b)")).then_inc(o_st[s], 16)
            pairs(act, n_tiles // 2, body)
            for s in range(2):
                act.wait_ge(o_st[s], 16 * (n_tiles // 2))

        @block.vector
        def _(dve):
            dve.sem_inc(xt_out, 1)
            dve.sem_inc(o_out, 1)
            dve.sem_inc(hh, 1)

            def out_x(i, s):
                t = 2 * i + s
                dve.wait_ge(xt_psum, t + 3)
                dve.wait_ge(ab, 2 * t) if not (isinstance(t, int) and t == 0) else None
                dve.tensor_copy(xT[:, 4:8, :], pX[:, 4:8, :]).then_inc(xt_out, 1)

            out_x(0, 0)

            def body(i, first, last):
                for s in range(2):
                    t = 2 * i + s
                    dve.wait_ge(ab, 2 * t + 2)
                    dve.wait_ge(sil, t + 1)
                    dve.tensor_tensor(h[:], h[:], pB[:], ALU.mult).then_inc(hh, 1)
                    if not (last and s == 1):
                        out_x(*at(i, s, 1))
                    dve.wait_ge(o_psum, 2 * t + 2)
                    dve.wait_ge(o_st[s], 16 * i) if not (isinstance(i, int) and i == 0) else None
                    dve.tensor_copy(ob[s][:, 1, :], pO[:, 1, :]).then_inc(o_out, 1)
            pairs(dve, n_tiles // 2, body)



def combine(core, ident, tag, layer, pos, wts, o_dram, x1_dram, mod_dram, gain_src, x2_dram=None, hnT_dram=None,
            out=None):
    nc = core.nc
    last_layer = out is not None
    sem = lambda name, n=None: core.sem(f"{tag}_{name}", n)
    const_ld, x_ld, o_ld = sem("const_loaded"), sem("x_loaded", 2), sem("rows_loaded", 2)
    ix_ready, gath, scaled, step = sem("idx_ready"), sem("gathers"), sem("scaled"), sem("dve_step")
    summed, squares, std, eps_set = sem("summed"), sem("squares"), sem("std"), sem("eps_set")
    x_st, hn_ready, tp, t_out, t_st = sem("x_stored", 2), sem("hn_ready", 2), sem("transposed"), sem("hT_out", 2), sem("hT_stored", 2)
    with ExitStack() as ctx:
        sb = lambda name, shape, dt=F32: core.sb(ctx, f"{tag}_{name}", shape, dt)
        sbs = lambda name, n, shape, dt=F32: core.sbs(ctx, f"{tag}_{name}", n, shape, dt)
        gate2, gain, shift, scale = sb("gate2", [P, D]), sb("gain", [P, D]), sb("shift", [P, D]), sb("scale", [P, D])
        ix = [sbs(f"idx{s}_", 2, [P, 1], I32) for s in range(2)]
        og = [sbs(f"rows{s}_", 2, [P, D]) for s in range(2)]
        xb, hn = sbs("x", 2, [P, D]), sbs("hn", 2, [P, D])
        junk = sb("junk", [P, D])
        eps = sb("eps", [P, 1])
        stat = sbs("stat", 2, [P, 4])
        hT = sbs("hT", 2, [P, KD, P])
        pT = [core.ps(ctx, f"{tag}_pT{s}", [P, KD, P]) for s in range(2)]
        block = ctx.enter_context(nc.Block())
        x1_view = x1_dram.rearrange("(n p) d -> n p d", p=P)
        if last_layer:
            out_view = out.rearrange("b (n p) d -> n p (b d)", p=P)
        else:
            x2_view = x2_dram.rearrange("(n p) d -> n p d", p=P)
            hT_view = hnT_dram.rearrange("(k p) (n f) -> n p k f", p=P, f=P)
        tile_of = lambda view, i, s: view[bass.ds(2 * i + s, 1)].squeeze(0)

        @block.sync
        def _(sp):
            def load(i, s):
                sp.dma_start(xb[s][:], tile_of(x1_view, i, s)).then_inc(x_ld[s], 16)

            def store(i, s):
                sp.wait_ge(hn_ready[s], i + 1)
                if last_layer:
                    sp.dma_start(tile_of(out_view, i, s), hn[s][:]).then_inc(x_st[s], 16)
                else:
                    sp.dma_start(tile_of(x2_view, i, s), xb[s][:]).then_inc(x_st[s], 16)
                    sp.wait_ge(t_out[s], i + 2)
                    sp.dma_start(tile_of(hT_view, i, s), hT[s][:]).then_inc(t_st[s], 16)

            sp.dma_start(gate2[:], row(mod_dram[layer:layer + 1, :], G2 * D, D)).then_inc(const_ld, 16)
            sp.dma_start(gain[:], row(gain_src, 0, D)).then_inc(const_ld, 16)
            if not last_layer:
                load_mod(sp, mod_dram, layer + 1, SC1, scale[:], const_ld)
                load_mod(sp, mod_dram, layer + 1, SH1, shift[:], const_ld)
            load(0, 0)
            load(0, 1)
            with sp.Fori(0, NT // 2 - 1) as i:
                for s in range(2):
                    store(i, s)
                    sp.wait_ge(x_st[s], 16 * i + 16)
                    load(i + 1, s)
            for s in range(2):
                store(NT // 2 - 1, s)
            for s in range(2):
                sp.wait_ge(x_st[s], 16 * (NT // 2))
                if not last_layer:
                    sp.wait_ge(t_st[s], 16 * (NT // 2))

        @block.gpsimd
        def _(pool):
            with pool.Fori(0, NT // 2) as i:
                for s in range(2):
                    n = 2 * i + s
                    pool.wait_ge(summed, n + 1)
                    for k in range(2):
                        pool.tensor_copy(ix[s][k][:], pos[:, bass.ds(n, 1), k]).then_inc(ix_ready, 1)
                    pool.wait_ge(ix_ready, 2 * n + 2)
                    pool.sem_inc(gath, 1)
                    for k in range(2):
                        pool.indirect_dma_start(og[s][k][:], None, o_dram,
                                                bass.IndirectOffsetOnAxis(ap=ix[s][k][:, 0:1], axis=0)) \
                            .then_inc(o_ld[s], 16)

        @block.scalar
        def _(act):
            if not last_layer:
                for s in range(2):
                    act.sem_inc(t_out[s], 1)

            def scale_first(i, s):
                act.wait_ge(o_ld[s], 32 * i + 32)
                act.activation(og[s][0][:], og[s][0][:], ACT.Copy, scale=wts[:, bass.ds(2 * i + s, 1), 0]) \
                   .then_inc(scaled, 1)

            def std_of(i, s):
                n = 2 * i + s
                act.wait_ge(summed, n + 3)
                act.activation(junk[:], xb[s][:], ACT.Square, accum_out=stat[s][:, 0:1]).then_inc(squares, 1)
                act.wait_ge(squares, n + 1)
                act.activation(stat[s][:, 1:2], stat[s][:, 0:1], ACT.Sqrt, scale=1.0 / D, bias=eps[:, 0:1]) \
                   .then_inc(std, 1)

            def out_t(i, s):
                act.wait_ge(tp, 2 * i + s + 3)
                if not (isinstance(i, int) and i == 0):
                    act.wait_ge(t_st[s], 16 * i)
                act.activation(hT[s][:], pT[s][:], ACT.Copy).then_inc(t_out[s], 1)

            act.wait_ge(eps_set, 1)
            scale_first(0, 0)

            def body(i, first, last):
                for s in range(2):
                    if not (last and s == 1):
                        scale_first(*at(i, s, 1))
                    std_of(i, s)
                    if not last_layer and not (first and s == 0):
                        out_t(*at(i, s, -1))
            pairs(act, NT // 2, body)
            if not last_layer:
                out_t(NT // 2 - 1, 1)

        if not last_layer:
            @block.tensor
            def _(pe):
                pe.sem_inc(tp, 2)
                with pe.Fori(0, NT // 2) as i:
                    for s in range(2):
                        pe.wait_ge(hn_ready[s], i + 1)
                        pe.wait_ge(t_out[s], i + 1)
                        for k in range(KD):
                            last = pe.transpose(pT[s][:, k, :], hn[s][:, k * P:(k + 1) * P], ident[:])
                        last.then_inc(tp, 1)

        @block.vector
        def _(dve):
            dve.memset(eps[:], EPS).then_inc(eps_set, 1)
            dve.wait_ge(const_ld, 32 if last_layer else 64)
            c = Chain(dve, step)
            c(dve.tensor_scalar(gate2[:], gate2[:], 1.0, None, ALU.add))
            if not last_layer:
                fold_scale(dve, c, gain[:], scale[:])
            base = c.n
            dve.sem_inc(summed, 2)
            stt, tt = dve.scalar_tensor_tensor, dve.tensor_tensor
            steps = 3 if last_layer else 4

            def add(i, s):
                n = 2 * i + s
                c = Chain(dve, step, base + (steps * n - (steps - 2) if not isinstance(n, int) or n else 0))
                dve.wait_ge(scaled, n + 1)
                dve.wait_ge(x_ld[s], 16 * i + 16)
                c(stt(out=og[s][0][:], in0=og[s][1][:], scalar=wts[:, bass.ds(n, 1), 1], in1=og[s][0][:],
                      op0=ALU.mult, op1=ALU.add))
                c(tt(og[s][0][:], og[s][0][:], gate2[:], ALU.mult))
                tt(xb[s][:], og[s][0][:], xb[s][:], ALU.add).then_inc(summed, 1)

            def norm(i, s):
                n = 2 * i + s
                c = Chain(dve, step, base + steps * n + 2 + (2 if not lastcall[0] else 0))
                dve.wait_ge(std, n + 1)
                if last_layer:
                    if not (isinstance(i, int) and i == 0):
                        dve.wait_ge(x_st[s], 16 * i)
                else:
                    dve.wait_ge(tp, n + 1)
                c(dve.reciprocal(stat[s][:, 2:3], stat[s][:, 1:2]))
                if last_layer:
                    stt(out=hn[s][:], in0=xb[s][:], scalar=stat[s][:, 2:3], in1=gain[:],
                        op0=ALU.mult, op1=ALU.mult).then_inc(hn_ready[s], 1)
                else:
                    c(stt(out=hn[s][:], in0=xb[s][:], scalar=stat[s][:, 2:3], in1=gain[:],
                          op0=ALU.mult, op1=ALU.mult))
                    tt(hn[s][:], hn[s][:], shift[:], ALU.add).then_inc(hn_ready[s], 1)

            lastcall = [False]
            add(0, 0)

            def body(i, first, last):
                for s in range(2):
                    if last and s == 1:
                        lastcall[0] = True
                    else:
                        add(*at(i, s, 1))
                    norm(i, s)
            pairs(dve, NT // 2, body)


def conv_in(core, tag, w_in, conv_w, hnT_dram, z_dram):
    nc = core.nc
    NC_, MC = 4, 2
    W = P * MC
    TB = T // HALF
    sem = lambda name, n=None: core.sem(f"{tag}_{name}", n)
    w_ld, w_hi_r, w_split, cw_ld = sem("w_loaded", 2), sem("w_hi"), sem("w_split"), sem("taps_loaded")
    r_ld, r_hi, r_lo = sem("r_loaded", 2), sem("r_hi"), sem("r_split")
    mm, c_out, used, step = sem("bank"), sem("c_out"), sem("banks_read"), sem("dve_step")
    z_ready, z_go, z_st = sem("z_ready"), sem("z_stores"), sem("z_stored", 2)
    with ExitStack() as ctx:
        sb = lambda name, shape, dt=F32: core.sb(ctx, f"{tag}_{name}", shape, dt)
        sbs = lambda name, n, shape, dt=F32: core.sbs(ctx, f"{tag}_{name}", n, shape, dt)
        w_raw, w_lo = zip(*[core.raw_low(ctx, f"{tag}_w{s}", [P, KD, 3, W]) for s in range(2)])
        x_raw, x_lo = zip(*[core.raw_low(ctx, f"{tag}_x{s}", [P, KD, HALF]) for s in range(2)])
        w_hi, x_hi = sbs("w_hi", 2, [P, KD, 3, W], F32R), sbs("x_hi", 2, [P, KD, HALF], F32R)
        taps = sb("taps", [P, 3, NC_ * MC])
        u = sbs("u", 2, [P, MC, HALF + 2])
        cs = sbs("c", MC, [P, HALF])
        z = sbs("z", MC, [P, HALF])
        pb = [[core.ps(ctx, f"{tag}_p{j}_{m}", [P, HALF]) for j in range(3)] for m in range(MC)]
        block = ctx.enter_context(nc.Block())
        w_view = w_in[0].rearrange("(k p) (j c f) -> c p k j f", p=P, j=3, f=W)
        x_view = hnT_dram.rearrange("(k p) (n f) -> n p k f", p=P, f=HALF)
        z_view = z_dram.rearrange("(c p) (n f) -> c n p f", p=P, f=HALF)

        @block.sync
        def _(sp):
            def weights(c):
                for k in range(KD):
                    sp.dma_start(w_raw[c % 2][:, k, :, :], w_view[c][:, k, :, :]).then_inc(w_ld[c % 2], 16)

            def load(r, t, s):
                sp.dma_start(x_raw[s][:], x_view[bass.ds(t, 1)].squeeze(0)).then_inc(r_ld[s], 16)

            sp.dma_start(taps[:], conv_w[0].rearrange("j (c p) -> p j c", p=P), allow_slow_non_contiguous=True) \
              .then_inc(cw_ld, 16)
            weights(0)
            for s in range(2):
                load(0, s, s)
            for c in range(NC_):
                if c + 1 < NC_:
                    if c >= 1:
                        sp.wait_ge(mm, 3 * MC * TB * c)
                    weights(c + 1)
                last = c == NC_ - 1
                with sp.Fori(0, TB // 2 - (1 if last else 0)) as i:
                    for s in range(2):
                        b = c * TB + 2 * i + s
                        sp.wait_ge(mm, 3 * MC * (b + 1))
                        load(None, (2 * i + s + 2) % TB, s)

        @block.scalar
        def _(act):
            def split_w(c):
                act.wait_ge(w_ld[c % 2], 16 * KD * (c // 2 + 1))
                for k in range(KD):
                    act.activation(w_hi[c % 2][:, k, :, :], w_raw[c % 2][:, k, :, :], ACT.Copy) \
                       .then_inc(w_hi_r, 1)

            def split_x(c, i, s):
                b = c * TB + 2 * i + s
                act.wait_ge(r_ld[s], 16 * (c * (TB // 2) + i + 1))
                if not isinstance(b, int) or b >= 2:
                    act.wait_ge(mm, 3 * MC * (b - 1))
                for h in range(2):
                    act.activation(x_hi[s][:, 4 * h:4 * h + 4, :], x_raw[s][:, 4 * h:4 * h + 4, :],
                                   ACT.Copy).then_inc(r_hi, 1)

            split_w(0)
            split_x(0, 0, 0)
            for c in range(NC_):
                if c + 1 < NC_:
                    split_w(c + 1)

                def body(i, first, last):
                    for s in range(2):
                        b = c * TB + 2 * i + s
                        if not (c == NC_ - 1 and last and s == 1):
                            split_x(c, *at(i, s, 1))
                        for m in range(MC):
                            act.wait_ge(mm, 3 * (MC * b + m) + 1)
                            act.wait_ge(used, MC * b + 1 + m)
                            act.activation(cs[m][:], pb[m][0][:], ACT.Copy).then_inc(c_out, 1)
                pairs(act, TB // 2, body)

        @block.tensor
        def _(pe):
            for c in range(NC_):
                pe.wait_ge(w_split, KD * (c + 1))
                with pe.Fori(0, TB // 2) as i:
                    for s in range(2):
                        b = c * TB + 2 * i + s
                        pe.wait_ge(r_lo, 2 * b + 2)
                        for m in range(MC):
                            pe.wait_ge(used, MC * b + 1 + m)
                            for n, j in enumerate((1, 2, 0)):
                                cols = slice(m * P, (m + 1) * P)
                                for k in range(KD):
                                    last = product(pe, pb[m][n][:], (w_hi[c % 2][:, k, j, cols], w_lo[c % 2][:, k, j, cols]),
                                                   (x_hi[s][:, k, :], x_lo[s][:, k, :]), k == 0, k == KD - 1)
                                last.then_inc(mm, 1)

        @block.gpsimd
        def _(pool):
            for c in range(NC_):
                with pool.Fori(0, TB) as n:
                    for m in range(MC):
                        b = c * TB + n
                        pool.wait_ge(z_ready, MC * b + m + 1)
                        pool.sem_inc(z_go, 1)
                        pool.dma_start(z_view[MC * c + m][bass.ds(n, 1)].squeeze(0), z[m][:]).then_inc(z_st[m], 16)
            for m in range(MC):
                pool.wait_ge(z_st[m], 16 * NC_ * TB)

        @block.vector
        def _(dve):
            dve.sem_inc(used, 2)
            dve.wait_ge(cw_ld, 16)

            def split_w(c):
                for k in range(KD):
                    dve.wait_ge(w_hi_r, KD * c + k + 1)
                    dve.tensor_tensor(w_lo[c % 2][:, k, :, :], w_raw[c % 2][:, k, :, :], w_hi[c % 2][:, k, :, :].bitcast(F32), ALU.subtract) \
                       .then_inc(w_split, 1)

            def split_x(c, i, s):
                b = c * TB + 2 * i + s
                for h in range(2):
                    dve.wait_ge(r_hi, 2 * b + h + 1)
                    dve.tensor_tensor(x_lo[s][:, 4 * h:4 * h + 4, :], x_raw[s][:, 4 * h:4 * h + 4, :], x_hi[s][:, 4 * h:4 * h + 4, :].bitcast(F32), ALU.subtract) \
                       .then_inc(r_lo, 1)

            per = 5
            split_w(0)
            split_x(0, 0, 0)
            for c in range(NC_):
                if c + 1 < NC_:
                    split_w(c + 1)
                base = c * (TB * MC * per + 1)
                Chain(dve, step, base)(dve.memset(u[0][:, :, 0:2], 0.0))
                base += 1

                def body(i, first, last):
                    for s in range(2):
                        b = c * TB + 2 * i + s
                        if not (c == NC_ - 1 and last and s == 1):
                            split_x(c, *at(i, s, 1))
                        for m in range(MC):
                            q = Chain(dve, step, base + ((2 * i + s) * MC + m) * per)
                            tap = lambda j: taps[:, j, MC * c + m:MC * c + m + 1]
                            dve.wait_ge(mm, 3 * (MC * b + m) + 2)
                            dve.wait_ge(c_out, MC * b + m + 1)
                            q(dve.tensor_tensor(u[s][:, m, 2:], cs[m][:], pb[m][1][:], ALU.mult))
                            q(dve.tensor_copy(u[1 - s][:, m, 0:2], u[s][:, m, HALF:HALF + 2]))
                            if not isinstance(b, int) or b >= 1:
                                dve.wait_ge(z_st[m], 16 * b)
                            q(dve.tensor_scalar(z[m][:], u[s][:, m, 0:HALF], tap(0), None, ALU.mult))
                            q(dve.scalar_tensor_tensor(out=z[m][:], in0=u[s][:, m, 1:HALF + 1], scalar=tap(1), in1=z[m][:],
                                                       op0=ALU.mult, op1=ALU.add))
                            q(dve.scalar_tensor_tensor(out=z[m][:], in0=u[s][:, m, 2:], scalar=tap(2), in1=z[m][:],
                                                       op0=ALU.mult, op1=ALU.add))
                            dve.wait_ge(mm, 3 * (MC * b + m) + 3)
                            dve.tensor_tensor(z[m][:], z[m][:], pb[m][2][:], ALU.mult).then_inc(z_ready, 1)
                            dve.wait_ge(z_ready, MC * b + m + 1)
                            dve.sem_inc(used, 1)
                pairs(dve, TB // 2, body)



def program(nc, x, c, ada_w, ada_b, norm1_g, norm2_g, ssm_w_in, ssm_lam_re, ssm_lam_im, ssm_log_dt, ssm_b_re,
            ssm_b_im, ssm_c_re, ssm_c_im, ssm_d, ssm_w_glu, conv_w_in, conv_w, conv_w_out, moe_wg, moe_bg, moe_we,
            moe_be, moe_w1, moe_w3, moe_w2, final_g, out):
    dram = lambda name, shape, dt=F32: nc.dram_tensor(name, shape, dt).ap()
    mod = dram("mod", [2, MOD])
    u = dram("u", [G, P, L * CH])
    y, hn, hnT, zT = dram("y", [T, D]), dram("hn", [T, D]), dram("hnT", [D, T]), dram("zT", [D, T])
    x1, x2 = dram("x1", [T, D]), dram("x2", [T, D])
    o = dram("expert_rows", [SLOTS, D])
    slots, tile_e = dram("slot_token", [SLOTS, 1], I32), dram("tile_expert", [P, 1], I32)
    rows = lambda a: a.rearrange("(n p) d -> n p d", p=P)
    with ExitStack() as ctx:
        core = Core(nc, ctx)
        ident = core.sb(ctx, "ident", [P, P])
        logits = core.sb(ctx, "logits", [P, NT, NL])
        pos, wts = core.sb(ctx, "pos", [P, NT, 2], I32), core.sb(ctx, "wts", [P, NT, 2])
        experts_row = core.sb(ctx, "experts_row", [1, P], I32)

        def moe(layer):
            core.phase(routing, f"r{layer}", logits, pos, wts, experts_row, slots, tile_e)
            core.phase(experts, ident, f"m{layer}", layer, moe_w1, moe_w3, moe_w2, experts_row, slots, hn, o)

        core.phase(constants, ident)
        core.phase(modulation, c, ada_w, ada_b, mod)
        core.phase(ssm_input, ident, x, norm1_g, ssm_w_in, mod, u)
        with ExitStack() as ssm:
            tab = SsmTables(core, ssm)
            core.phase(ssm_tables, ident, ssm_lam_re, ssm_lam_im, ssm_log_dt, ssm_b_re, ssm_b_im, ssm_c_re, ssm_c_im,
                       ssm_d, tab)
            core.phase(ssm_scan, ident, tab, u, y)
        core.phase(project, ident, "glu", 0, True, y, ssm_w_glu[0], x.rearrange("b (n p) d -> n p (b d)", p=P), norm2_g,
                moe_wg, moe_bg, moe_we, moe_be, mod, x1, hn, logits)
        moe(0)
        core.phase(combine, ident, "c0", 0, pos, wts, o, x1, mod, norm1_g[1:2, :], x2_dram=x2, hnT_dram=hnT)
        core.phase(conv_in, "conv", conv_w_in, conv_w, hnT, zT)
        core.phase(project, ident, "cout", 1, False, zT, conv_w_out[0], rows(x2), norm2_g,
                moe_wg, moe_bg, moe_we, moe_be, mod, x1, hn, logits)
        moe(1)
        core.phase(combine, ident, "c1", 1, pos, wts, o, x1, mod, final_g.rearrange("(a d) -> a d", a=1), out=out)


_INS = ["x", "c", "ada_w", "ada_b", "norm1_g", "norm2_g", "ssm_w_in", "ssm_lam_re", "ssm_lam_im", "ssm_log_dt",
        "ssm_b_re", "ssm_b_im", "ssm_c_re", "ssm_c_im", "ssm_d", "ssm_w_glu", "conv_w_in", "conv_w", "conv_w_out",
        "moe_wg", "moe_bg", "moe_we", "moe_be", "moe_w1", "moe_w3", "moe_w2", "final_g"]
_OUTS = [((1, T, D), "float32")]


def kernel(**inputs):
    import numpy as _np
    import concourse.bacc as _bacc
    from concourse import mybir as _mybir
    from concourse.bass_utils import run_bass_kernel_spmd as _run

    nc = _bacc.Bacc("TRN2", target_bir_lowering=False, num_devices=1)
    arrays, args = {}, []
    for name in _INS:
        a = _np.ascontiguousarray(inputs[name])
        arrays[f"in_{name}_dram"] = a
        args.append(nc.dram_tensor(f"in_{name}_dram", a.shape, _mybir.dt.from_np(a.dtype), kind="ExternalInput").ap())
    for i, (shape, dtype) in enumerate(_OUTS):
        dt = _mybir.dt.from_np(_np.dtype(dtype))
        args.append(nc.dram_tensor(f"out_{i}_dram", shape, dt, kind="ExternalOutput").ap())
    program(nc, *args)
    r = _run(nc, [arrays], core_ids=[0])
    return r.results[0]["out_0_dram"]
```

```python
from contextlib import ExitStack

import numpy as np
import concourse.bass as bass
from concourse import mybir

F32 = mybir.dt.float32
F32R = mybir.dt.float32r
I32 = mybir.dt.int32
ALU = mybir.AluOpType
ACT = mybir.ActivationFunctionType
AX = mybir.AxisListType

P = 128
D = 1024
KD = D // P
T = 4096
NT = T // P
HALF = 512
L = T // P
G, S, CH = 64, 64, 16
KB = L * CH // P
SB = L // KB
LEVELS = 7
NG, EG, NE = 4, 8, 32
FE = 512
KF = FE // P
TILES = 2 * T // P + NE - 1
SLOTS = (TILES + 1) * P
EPS = 1e-6
MOD = 6 * D
SH1, SC1, G1, SH2, SC2, G2 = range(6)


class Chain:

    def __init__(self, eng, sem, base=0):
        self.eng, self.sem, self.base, self.n = eng, sem, base, 0

    def __call__(self, ins):
        self.n += 1
        ins.then_inc(self.sem, 1)
        self.eng.wait_ge(self.sem, self.base + self.n)


def at(i, s, d=0, slots=2):
    return i + (s + d) // slots, (s + d) % slots


def pairs(eng, n, body):
    body(0, True, False)
    with eng.Fori(1, n - 1) as i:
        body(i, False, False)
    body(n - 1, False, True)


class Core:

    def __init__(self, nc, ctx):
        self.nc, self.ctx = nc, ctx

    def sem(self, name, n=None):
        if n is None:
            return self.nc.alloc_semaphore(name)
        return [self.nc.alloc_semaphore(f"{name}{i}") for i in range(n)]

    def phase(self, build, *args, **kw):
        with self.nc.cleanup_on_exit():
            build(self, *args, **kw)

    def sb(self, ctx, name, shape, dt=F32):
        return ctx.enter_context(self.nc.sbuf_tensor(name, shape, dt))

    def sbs(self, ctx, name, n, shape, dt=F32):
        return [self.sb(ctx, f"{name}{i}", shape, dt) for i in range(n)]

    def raw_low(self, ctx, name, shape):
        at_byte = -(-self.nc.sbuf_base // 32) * 32
        raw = self.sb(ctx, name + "_raw", shape)
        return raw, self.nc.alloc_sbuf_tensor_at(name + "_lo", shape, F32R, offset=at_byte)

    def ps(self, ctx, name, shape):
        return ctx.enter_context(self.nc.psum_tensor(name, shape, F32))


def product(pe, out, lhs, rhs, start, stop):
    (lh, ll), (rh, rl) = lhs, rhs
    pe.matmul(out, lh, rl, start=start, stop=False)
    pe.matmul(out, ll, rh, start=False, stop=False)
    return pe.matmul(out, lh, rh, start=False, stop=stop)


def row(ap, a, n):
    return ap[:, a:a + n].broadcast_to([P, n])



def constants(core, ident):
    nc = core.nc
    step = core.sem("ident_step")
    with nc.Block() as block:
        @block.gpsimd
        def _(pool):
            c = Chain(pool, step)
            c(pool.memset(ident[:], 0.0))
            c(pool.affine_select(out=ident[:], in_=ident[:], compare_op=ALU.not_equal, fill=1.0,
                                 base=0, pattern=[[-1, P]], channel_multiplier=1))


class Modulation:

    ROUNDS = MOD // HALF // 2

    def __init__(self, core, ctx, layer, c_in, ada_w, ada_b, mod_dram):
        tag = f"mod{layer}"
        self.c_in, self.bias_src, self.dst = c_in, ada_b[layer:layer + 1, :], mod_dram[layer:layer + 1, :]
        self.w_view = ada_w[layer].rearrange("(k p) n -> p k n", p=P)
        self.c_ld, self.b_ld, self.w_ld = core.sem(f"{tag}_c_loaded"), core.sem(f"{tag}_b_loaded"), core.sem(f"{tag}_w_loaded", 2)
        self.cond_ready, self.mm, self.out = core.sem(f"{tag}_cond"), core.sem(f"{tag}_product", 2), core.sem(f"{tag}_out", 2)
        self.added, self.st = core.sem(f"{tag}_added"), core.sem(f"{tag}_stored")
        self.cond_sb = core.sb(ctx, f"{tag}_cond_sb", [P, 2, KD])
        self.w = core.sbs(ctx, f"{tag}_w", 2, [P, KD, HALF])
        self.bias, self.row = core.sb(ctx, f"{tag}_bias", [1, MOD]), core.sb(ctx, f"{tag}_row", [1, MOD])
        self.ps = [core.ps(ctx, f"{tag}_ps{s}", [P, HALF]) for s in range(2)]

    def load(self, sp, i, s):
        sp.wait_ge(self.mm[s], i + 1)
        sp.dma_start(self.w[s][:], self.w_view[:, :, bass.ts(2 * i + s, HALF)]).then_inc(self.w_ld[s], 16)

    def first_loads(self, sp):
        sp.dma_start(self.cond_sb[:, 0, :], self.c_in.rearrange("b (k p) -> p (b k)", p=P),
                     allow_slow_non_contiguous=True).then_inc(self.c_ld, 16)
        sp.dma_start(self.bias[:], self.bias_src).then_inc(self.b_ld, 16)
        self.load(sp, 0, 0)
        self.load(sp, 0, 1)

    def loads(self, sp):
        with sp.Fori(1, self.ROUNDS) as i:
            self.load(sp, i, 0)
            self.load(sp, i, 1)

    def store(self, sp):
        sp.wait_ge(self.added, 2 * self.ROUNDS)
        sp.dma_start(self.dst, self.row[:]).then_inc(self.st, 16)
        sp.wait_ge(self.st, 16)

    def cond(self, act):
        act.wait_ge(self.c_ld, 16)
        act.activation(self.cond_sb[:, 1, :], self.cond_sb[:, 0, :], ACT.Silu).then_inc(self.cond_ready, 1)
        for s in range(2):
            act.sem_inc(self.out[s], 1)

    def start(self, pe):
        for s in range(2):
            pe.sem_inc(self.mm[s], 1)
        pe.wait_ge(self.cond_ready, 1)

    def products(self, pe, a, b):
        with pe.Fori(a, b) as i:
            for s in range(2):
                pe.wait_ge(self.w_ld[s], 16 * i + 16)
                pe.wait_ge(self.out[s], i + 1)
                for k in range(KD):
                    last = pe.matmul(self.ps[s][0:1, :], self.cond_sb[:, 1, k:k + 1], self.w[s][:, k, :],
                                     start=k == 0, stop=k == KD - 1)
                last.then_inc(self.mm[s], 1)

    def results(self, act):
        with act.Fori(0, self.ROUNDS) as i:
            for s in range(2):
                act.wait_ge(self.mm[s], i + 2)
                act.activation(self.row[0:1, bass.ts(2 * i + s, HALF)], self.ps[s][0:1, :], ACT.Copy) \
                   .then_inc(self.out[s], 1)

    def biases(self, dve):
        dve.wait_ge(self.b_ld, 16)
        with dve.Fori(0, self.ROUNDS) as i:
            for s in range(2):
                dve.wait_ge(self.out[s], i + 2)
                c = bass.ts(2 * i + s, HALF)
                dve.tensor_tensor(self.row[0:1, c], self.row[0:1, c], self.bias[0:1, c], ALU.add).then_inc(self.added, 1)



def load_mod(sp, mod_dram, layer, which, dst, sem):
    sp.dma_start(dst, row(mod_dram[layer:layer + 1, :], which * D, D)).then_inc(sem, 16)


def fold_scale(dve, chain, gain, scale):
    chain(dve.scalar_tensor_tensor(out=gain, in0=scale, scalar=1.0, in1=gain, op0=ALU.add, op1=ALU.mult))



def ssm_input(core, ident, x, norm_g, w_in, mod_dram, u_dram):
    nc = core.nc
    BLK = 8
    x_view = x.rearrange("b (c t) d -> t c (b d)", t=L)
    u_view = u_dram.rearrange("g c (n f) -> n c g f", f=BLK * CH)
    const_ld, w_ld, x_ld = core.sem("a_const_loaded"), core.sem("a_w_loaded", KD), core.sem("a_x_loaded", 2)
    w_hi_ready, w_ready = core.sem("a_w_hi_ready"), core.sem("a_w_split")
    step, var, std = core.sem("a_dve_step"), core.sem("a_var_ready", 2), core.sem("a_std_ready", 2)
    hn_ready = core.sem("a_hn_ready", 2)
    tp, thi, tlo = core.sem("a_transposed", 2), core.sem("a_hT_hi", 2), core.sem("a_hT_lo", 2)
    mm, ev = core.sem("a_product", 2), core.sem("a_evacuated", 2)
    blk_ready, blk_stored = core.sem("a_block_ready"), core.sem("a_block_stored")
    stage_free = core.sem("a_stage_free")
    with ExitStack() as ctx:
        gain, shift = core.sb(ctx, "a_gain", [P, D]), core.sb(ctx, "a_shift", [P, D])
        scale = core.sb(ctx, "a_scale", [P, D])
        w_raw, w_lo = core.raw_low(ctx, "a_w", [P, KD, D])
        w_hi = core.sb(ctx, "a_w_hi", [P, KD, D], F32R)
        xb = core.sbs(ctx, "a_x", 2, [P, D])
        hn = core.sbs(ctx, "a_hn", 2, [P, D])
        stat = core.sbs(ctx, "a_stat", 2, [P, 4])
        h_hi = core.sbs(ctx, "a_hT_hi", 2, [P, KD, P], F32R)
        h_lo = core.sbs(ctx, "a_hT_lo", 2, [P, KD, P], F32R)
        stage = core.sb(ctx, "a_stage", [P, G, BLK * CH])
        pT = [core.ps(ctx, f"a_pT{s}", [P, KD, P]) for s in range(2)]
        pU = [core.ps(ctx, f"a_pU{s}", [P, 2, HALF]) for s in range(2)]
        stage_v = stage[:].rearrange("p g (t f) -> p g t f", f=CH)
        block = ctx.enter_context(nc.Block())

        @block.sync
        def _(sp):
            sp.dma_start(gain[:], row(norm_g[0:1, :], 0, D)).then_inc(const_ld, 16)
            load_mod(sp, mod_dram, 0, SC1, scale[:], const_ld)
            load_mod(sp, mod_dram, 0, SH1, shift[:], const_ld)
            for s in range(2):
                sp.dma_start(xb[s][:], x_view[s]).then_inc(x_ld[s], 16)
            for k in range(KD):
                sp.dma_start(w_raw[:, k, :], w_in[0].rearrange("(k p) n -> k p n", p=P)[k]).then_inc(w_ld[k], 16)
            with sp.Fori(1, NT // 2) as i:
                for s in range(2):
                    sp.wait_ge(hn_ready[s], i)
                    sp.dma_start(xb[s][:], x_view[bass.ds(2 * i + s, 1)].squeeze(0)).then_inc(x_ld[s], 16)

        @block.gpsimd
        def _(pool):
            pool.sem_inc(stage_free, 1)
            with pool.Fori(0, NT // BLK) as n:
                pool.wait_ge(blk_ready, BLK * n + BLK)
                pool.dma_start(u_view[bass.ds(n, 1)].squeeze(0), stage[:]).then_inc(blk_stored, 16)
                pool.wait_ge(blk_stored, 16 * n + 16)
                pool.sem_inc(stage_free, 1)

        @block.vector
        def _(dve):
            dve.wait_ge(const_ld, 48)
            chain = Chain(dve, step)
            fold_scale(dve, chain, gain[:], scale[:])
            base = chain.n

            def norm(i, s):
                dve.wait_ge(x_ld[s], 16 * i + 16)
                dve.wait_ge(tp[s], i + 1)
                c = Chain(dve, step, base + 6 * i + 3 * s)
                c(dve.tensor_tensor_reduce(out=hn[s][:], in0=xb[s][:], in1=xb[s][:], scale=1.0, scalar=0.0,
                                           op0=ALU.mult, op1=ALU.add, accum_out=stat[s][:, 0:1]))
                dve.tensor_scalar(stat[s][:, 1:2], stat[s][:, 0:1], 1.0 / D, EPS, ALU.mult, ALU.add) \
                   .then_inc(var[s], 1)
                dve.wait_ge(std[s], i + 1)
                c(dve.reciprocal(stat[s][:, 3:4], stat[s][:, 2:3]))
                c(dve.scalar_tensor_tensor(out=hn[s][:], in0=xb[s][:], scalar=stat[s][:, 3:4], in1=gain[:],
                                           op0=ALU.mult, op1=ALU.mult))
                dve.tensor_tensor(hn[s][:], hn[s][:], shift[:], ALU.add).then_inc(hn_ready[s], 1)

            def low(i, s):
                dve.wait_ge(thi[s], 2 * i + 2)
                dve.tensor_tensor(h_lo[s][:], pT[s][:], h_hi[s][:].bitcast(F32), ALU.subtract) \
                   .then_inc(tlo[s], 1)

            norm(0, 0)
            low(0, 0)
            norm(0, 1)
            for k in range(KD):
                dve.wait_ge(w_hi_ready, k + 1)
                dve.tensor_tensor(w_lo[:, k, :], w_raw[:, k, :], w_hi[:, k, :].bitcast(F32), ALU.subtract) \
                   .then_inc(w_ready, 1)

            def body(i, first, last):
                for s in range(2):
                    if not (last and s == 1):
                        low(*at(i, s, 1))
                    if not last:
                        norm(*at(i, s, 2))
            pairs(dve, NT // 2, body)

        @block.tensor
        def _(pe):
            for s in range(2):
                pe.sem_inc(tp[s], 1)
                pe.sem_inc(mm[s], 2)

            def transposes(i, s):
                pe.wait_ge(hn_ready[s], i + 1)
                pe.wait_ge(tlo[s], i + 1)
                for k in range(KD):
                    last = pe.transpose(pT[s][:, k, :], hn[s][:, k * P:(k + 1) * P], ident[:])
                last.then_inc(tp[s], 1)

            def products(i, s):
                pe.wait_ge(tlo[s], i + 2)
                pe.wait_ge(ev[s], 2 * i + 2)
                for n in range(2):
                    for k in range(KD):
                        if isinstance(i, int) and i + s + n == 0:
                            pe.wait_ge(w_ready, k + 1)
                        last = product(pe, pU[s][:, n, :], (h_hi[s][:, k, :], h_lo[s][:, k, :]),
                                       (w_hi[:, k, bass.ts(n, HALF)], w_lo[:, k, bass.ts(n, HALF)]),
                                       k == 0, k == KD - 1)
                    last.then_inc(mm[s], 1)

            transposes(0, 0)

            def body(i, first, last):
                for s in range(2):
                    if not (last and s == 1):
                        transposes(*at(i, s, 1))
                    products(i, s)
            pairs(pe, NT // 2, body)

        @block.scalar
        def _(act):
            for s in range(2):
                act.sem_inc(tlo[s], 1)
                act.sem_inc(ev[s], 2)

            def std_of(i, s):
                act.wait_ge(var[s], i + 1)
                act.activation(stat[s][:, 2:3], stat[s][:, 1:2], ACT.Sqrt).then_inc(std[s], 1)

            def high(i, s):
                act.wait_ge(tp[s], i + 2)
                act.wait_ge(mm[s], 2 * i + 2)
                for h in range(2):
                    act.activation(h_hi[s][:, 4 * h:4 * h + 4, :], pT[s][:, 4 * h:4 * h + 4, :], ACT.Copy) \
                       .then_inc(thi[s], 1)

            def evacuate(i, s):
                t = 2 * i + s
                act.wait_ge(stage_free, t // BLK + 1)
                for n in range(2):
                    act.wait_ge(mm[s], 2 * i + n + 3)
                    act.activation(stage_v[:, n * 32:n * 32 + 32, bass.ds(t % BLK, 1), :].squeeze(2),
                                   pU[s][:, n, :].rearrange("p (g f) -> p g f", f=CH), ACT.Copy) \
                       .then_inc(ev[s], 1)
                act.wait_ge(ev[s], 2 * i + 4)
                act.sem_inc(blk_ready, 1)

            std_of(0, 0)
            high(0, 0)
            std_of(0, 1)
            for k in range(KD):
                act.wait_ge(w_ld[k], 16)
                act.activation(w_hi[:, k, :], w_raw[:, k, :], ACT.Copy).then_inc(w_hi_ready, 1)

            def body(i, first, last):
                for s in range(2):
                    if not (last and s == 1):
                        high(*at(i, s, 1))
                    if not last:
                        std_of(*at(i, s, 2))
                    evacuate(i, s)
            pairs(act, NT // 2, body)


def ssm_tables(core, ident, lam_re, lam_im, log_dt, b_re, b_im, c_re, c_im, d_skip, tab, *mod_args):
    nc = core.nc
    TWO_PI = 2 * np.pi
    C1 = 6.28125
    C2 = float(np.float32(TWO_PI - C1))
    ld = core.sem("t_loaded")
    step, pre, tp = core.sem("t_dve_step"), core.sem("t_rows_ready"), core.sem("t_transposed")
    to_act, to_dve = core.sem("t_for_act"), core.sem("t_from_act")
    sw = core.sem("t_swap_step")
    with ExitStack() as ctx:
        lam = core.sb(ctx, "t_lam", [P, 2, S])
        crow = core.sb(ctx, "t_crow", [P, 2, 8, 2, S])
        lt = core.sb(ctx, "t_lamT", [P, 2, G])
        dt_b = core.sb(ctx, "t_dt", [P, G])
        X, Y = core.sb(ctx, "t_bx", [P, G, CH]), core.sb(ctx, "t_by", [P, G, CH])
        tmp, tmp2 = core.sb(ctx, "t_tmp", [P, G, CH]), core.sb(ctx, "t_tmp2", [P, G, CH])
        ab = core.sb(ctx, "t_ab", [P, 14, G])
        ki = core.sb(ctx, "t_turns", [P, G], I32)
        sg = core.sb(ctx, "t_sign", [P, 1])
        ps_l = core.ps(ctx, "t_pl", [P, 2, G])
        ps_c = [core.ps(ctx, f"t_pc{n}", [P, 8, P]) for n in range(2)]
        mod = Modulation(core, ctx, 0, *mod_args)
        block = ctx.enter_context(nc.Block())
        lr, li = lt[:, 0, :], lt[:, 1, :]

        @block.sync
        def _(sp):
            mod.first_loads(sp)
            def get(dst, src, slow=False):
                sp.dma_start(dst, src, allow_slow_non_contiguous=slow).then_inc(ld, 16)
            for h in range(2):
                get(lam[0:S, h, :], lam_re[0])
                get(lam[S:P, h, :], lam_im[0])
                hs = slice(h * S, h * S + S)
                get(X[hs], (b_re, b_im)[h][0].rearrange("g p c -> p g c"))
                get(Y[hs], (b_im, b_re)[h][0].rearrange("g p c -> p g c"))
                for n, src in enumerate(((c_re, c_im), (c_im, c_re))):
                    get(crow[:, n, :, h, :], src[h][0].rearrange("(a g) c p -> (g c) a p", g=8))
            get(dt_b[:], log_dt.broadcast_to([P, G]))
            for i in range(SB):
                get(tab.skip[i * CH:(i + 1) * CH, :], d_skip[0].rearrange("(g c) -> c g", c=CH), True)
            mod.loads(sp)
            mod.store(sp)

        loads = 16 * (12 + 1 + SB)

        @block.gpsimd
        def _(pool):
            c = Chain(pool, sw)
            c(pool.memset(tab.swap[:], 0.0))
            for off in (-S, S):
                c(pool.affine_select(out=tab.swap[:], in_=tab.swap[:], compare_op=ALU.not_equal, fill=1.0,
                                     base=off, pattern=[[-1, P]], channel_multiplier=1))

        @block.tensor
        def _(pe):
            mod.start(pe)
            mod.products(pe, 0, 1)
            pe.wait_ge(ld, loads)
            pe.transpose(ps_l[:].rearrange("p a g -> p (a g)"), lam[:].rearrange("p a s -> p (a s)"), ident[:])
            pe.wait_ge(pre, 1)
            for n in range(2):
                for a in range(8):
                    last = pe.transpose(ps_c[n][:, a, :], crow[:, n, a, :, :].rearrange("p h s -> p (h s)"), ident[:])
            last.then_inc(tp, 1)
            mod.products(pe, 1, mod.ROUNDS)

        @block.scalar
        def _(act):
            mod.cond(act)
            act.wait_ge(to_act, 1)
            act.activation(ab[:, 0, :], dt_b[:], ACT.Exp).then_inc(to_dve, 1)
            act.wait_ge(to_act, 2)
            act.activation(ab[:, 2, :], ab[:, 1, :], ACT.Exp).then_inc(to_dve, 1)
            act.wait_ge(to_act, 3)
            act.activation(ab[:, 4, :], ab[:, 3, :], ACT.Sin)
            act.activation(ab[:, 5, :], ab[:, 3, :], ACT.Sin, scale=0.5).then_inc(to_dve, 1)
            mod.results(act)

        @block.vector
        def _(dve):
            c = Chain(dve, step)
            tt, ts, stt = dve.tensor_tensor, dve.tensor_scalar, dve.scalar_tensor_tensor
            dve.wait_ge(ld, loads)
            c(ts(crow[:, 0, :, 1, :], crow[:, 0, :, 1, :], -1.0, None, ALU.mult))
            c(ts(crow[:, 1, :, :, :], crow[:, 1, :, :, :], -1.0, None, ALU.mult))
            dve.sem_inc(pre, 1)
            dve.sem_inc(to_act, 1)
            c(dve.memset(sg[0:S, :], -1.0))
            c(dve.memset(sg[S:P, :], 1.0))
            dve.wait_ge(tp, 1)
            c(dve.tensor_copy(lt[:], ps_l[:]))
            for n, dst in enumerate((tab.c1, tab.c2)):
                c(dve.tensor_copy(dst[:], ps_c[n][:].rearrange("p a (g c) -> p (a g) c", c=CH)))
            dve.wait_ge(to_dve, 1)
            c(tt(ab[:, 1, :], lr, ab[:, 0, :], ALU.mult))
            dve.sem_inc(to_act, 1)
            c(tt(ab[:, 6, :], li, ab[:, 0, :], ALU.mult))
            c(ts(ab[:, 7, :], ab[:, 6, :], 1 / TWO_PI, None, ALU.mult))
            c(dve.tensor_copy(ki[:], ab[:, 7, :]))
            c(dve.tensor_copy(ab[:, 7, :], ki[:]))
            c(stt(out=ab[:, 6, :], in0=ab[:, 7, :], scalar=-C1, in1=ab[:, 6, :], op0=ALU.mult, op1=ALU.add))
            c(stt(out=ab[:, 6, :], in0=ab[:, 7, :], scalar=-C2, in1=ab[:, 6, :], op0=ALU.mult, op1=ALU.add))
            for cmp, turn in ((ALU.is_gt, -TWO_PI), (ALU.is_lt, TWO_PI)):
                c(ts(ab[:, 7, :], ab[:, 6, :], float(np.float32(np.pi)) * (1 if cmp == ALU.is_gt else -1), turn,
                     cmp, ALU.mult))
                c(tt(ab[:, 6, :], ab[:, 6, :], ab[:, 7, :], ALU.add))
            c(ts(ab[:, 3, :], ab[:, 6, :], 3.1415925, -3.1415925, ALU.min, ALU.max))
            dve.sem_inc(to_act, 1)
            dve.wait_ge(to_dve, 3)
            c(tt(ab[:, 6, :], ab[:, 5, :], ab[:, 5, :], ALU.mult))
            c(ts(ab[:, 6, :], ab[:, 6, :], -2.0, 1.0, ALU.mult, ALU.add))
            c(dve.memset(tab.pr[:, :, 0:1], 1.0))
            c(dve.memset(tab.pi[:, :, 0:1], 0.0))
            ar, ai = tab.pr[:, :, 1], tab.pi[:, :, 1]
            c(tt(ar, ab[:, 2, :], ab[:, 6, :], ALU.mult))
            c(tt(ai, ab[:, 2, :], ab[:, 4, :], ALU.mult))
            c(tt(ab[:, 7, :], lr, lr, ALU.mult))
            c(tt(ab[:, 8, :], li, li, ALU.mult))
            c(tt(ab[:, 7, :], ab[:, 7, :], ab[:, 8, :], ALU.add))
            c(dve.reciprocal(ab[:, 8, :], ab[:, 7, :]))
            c(ts(ab[:, 9, :], ar, -1.0, None, ALU.add))
            c(tt(ab[:, 10, :], ab[:, 9, :], lr, ALU.mult))
            c(tt(ab[:, 11, :], ai, li, ALU.mult))
            c(tt(ab[:, 10, :], ab[:, 10, :], ab[:, 11, :], ALU.add))
            c(tt(ab[:, 10, :], ab[:, 10, :], ab[:, 8, :], ALU.mult))
            c(tt(ab[:, 11, :], ai, lr, ALU.mult))
            c(tt(ab[:, 12, :], ab[:, 9, :], li, ALU.mult))
            c(tt(ab[:, 11, :], ab[:, 11, :], ab[:, 12, :], ALU.subtract))
            c(tt(ab[:, 11, :], ab[:, 11, :], ab[:, 8, :], ALU.mult))
            wide = lambda a: a.unsqueeze(2).broadcast_to([P, G, CH])
            cfr, cfi = wide(ab[:, 10, :]), wide(ab[:, 11, :])
            c(tt(tab.b1[:], X[:], cfr, ALU.mult))
            c(tt(tmp[:], Y[:], cfi, ALU.mult))
            c(stt(out=tab.b1[:], in0=tmp[:], scalar=sg[:, 0:1], in1=tab.b1[:], op0=ALU.mult, op1=ALU.add))
            c(tt(tmp[:], X[:], cfi, ALU.mult))
            c(tt(tmp2[:], Y[:], cfr, ALU.mult))
            c(stt(out=tab.b2[:], in0=tmp2[:], scalar=sg[:, 0:1], in1=tmp[:], op0=ALU.mult, op1=ALU.subtract))
            m = 1
            q1, q2 = tmp, tmp2
            while m < L:
                sr, si = tab.pr[:, :, 1:m + 1], tab.pi[:, :, 1:m + 1]
                mr = tab.pr[:, :, m:m + 1].broadcast_to([P, G, m])
                mi = tab.pi[:, :, m:m + 1].broadcast_to([P, G, m])
                dr, di = tab.pr[:, :, m + 1:2 * m + 1], tab.pi[:, :, m + 1:2 * m + 1]
                a, b = q1[:, :, 0:m], q2[:, :, 0:m]
                c(tt(dr, sr, mr, ALU.mult))
                c(tt(a, si, mi, ALU.mult))
                c(tt(di, sr, mi, ALU.mult))
                c(tt(b, si, mr, ALU.mult))
                c(tt(dr, dr, a, ALU.subtract))
                c(tt(di, di, b, ALU.add))
                m *= 2
            c(dve.tensor_copy(tab.back_r[:], tab.pr[:, :, L - 1::-1]))
            c(dve.tensor_copy(tab.back_i[:], tab.pi[:, :, L - 1::-1]))
            hr, hi = tab.ha, tab.hb
            c(dve.tensor_copy(hr[:, :, 0], tab.pr[:, :, L]))
            c(dve.tensor_copy(hi[:, :, 0], tab.pi[:, :, L]))
            for k in range(1, LEVELS):
                c(tt(ab[:, 0, :], hi[:, :, k - 1], hi[:, :, k - 1], ALU.mult))
                c(tt(hr[:, :, k], hr[:, :, k - 1], hr[:, :, k - 1], ALU.mult))
                c(tt(hr[:, :, k], hr[:, :, k], ab[:, 0, :], ALU.subtract))
                c(stt(out=hi[:, :, k], in0=hr[:, :, k - 1], scalar=2.0, in1=hi[:, :, k - 1],
                      op0=ALU.mult, op1=ALU.mult))
            c(ts(hi[:], hi[:], sg[:, 0:1], -1.0, ALU.mult, ALU.mult))
            mod.biases(dve)


def ssm_scan(core, ident, tab, u_dram, y_dram):
    nc = core.nc
    BG = 4
    NB = G // BG
    y_view = y_dram.rearrange("(c t) (n f) -> n c t f", t=L, f=2 * BG * CH)
    u_ld, pool_terms, terms_used = core.sem("s_u_loaded", 2), core.sem("s_pool_terms", 2), core.sem("s_terms_used", 2)
    tabs, zeroed = core.sem("s_tables", 2), core.sem("s_zeroed")
    ut_psum, ut_out = core.sem("s_uT_in_psum"), core.sem("s_uT_out")
    p_psum, p_out = core.sem("s_p_in_psum"), core.sem("s_p_out")
    r_psum, r_out = core.sem("s_r_in_psum"), core.sem("s_r_out")
    v_psum, diags, mats = core.sem("s_v_in_psum"), core.sem("s_diagonals"), core.sem("s_scan_matrices")
    copied, level = core.sem("s_scan_copied"), core.sem("s_scan_level")
    y_psum, y_out, y_st = core.sem("s_y_in_psum"), core.sem("s_y_out"), core.sem("s_y_stored")
    batch_done = core.sem("s_batch_done")
    vstep, ostep, tab_o = core.sem("s_dve_step"), core.sem("s_dve_step_o"), core.sem("s_table_o")
    with ExitStack() as ctx:
        us = core.sbs(ctx, "s_u", 2, [P, KB, P])
        t2o, t2p = core.sbs(ctx, "s_t2o", 2, [P, L + 1, CH]), core.sbs(ctx, "s_t2p", 2, [P, L, CH])
        pt = core.sbs(ctx, "s_pt", 2, [P, L, CH])
        z = core.sbs(ctx, "s_z", 2, [P, 2 * SB - 1, CH])
        pw = core.sbs(ctx, "s_p", 2, [P, KB, P])
        uT = [core.sbs(ctx, f"s_uT{b}_", BG, [P, KB, P]) for b in range(2)]
        O = [core.sbs(ctx, f"s_o{b}_", BG, [P, L + 1, CH]) for b in range(2)]
        R = [core.sbs(ctx, f"s_r{b}_", BG, [P, L, CH]) for b in range(2)]
        M = core.sbs(ctx, "s_m", 2, [P, BG, LEVELS, P])
        sc = core.sb(ctx, "s_copy", [P, BG, P])
        sx = core.sb(ctx, "s_before", [P, BG, P])
        stage = core.sb(ctx, "s_stage", [P, L, 2 * BG * CH])
        pU, pP, pR = core.ps(ctx, "s_pU", [P, KB, P]), core.ps(ctx, "s_pP", [P, KB, P]), core.ps(ctx, "s_pR", [P, L, CH])
        pV = [core.ps(ctx, f"s_pV{b}", [P, BG, P]) for b in range(2)]
        pY = [core.ps(ctx, f"s_pY{b}", [P, L, CH]) for b in range(2)]
        flat = lambda a: a.rearrange("p a b -> p (a b)")
        block = ctx.enter_context(nc.Block())

        def number(i, s, g):
            return (2 * i + s) * BG + g

        def turn(i, s, g):
            return (2 * i + s) * (BG // 2) + g // 2

        @block.sync
        def _(sp):
            def load(i, s):
                for g in range(BG):
                    n = number(i, s, g)
                    sp.wait_ge(ut_psum, n + 1)
                    sp.dma_start(flat(us[g % 2][:]), u_dram[bass.ds(n, 1)].squeeze(0)).then_inc(u_ld[g % 2], 16)

            load(0, 0)
            load(0, 1)
            with sp.Fori(0, NB // 2 - 1) as i:
                load(i + 1, 0)
                load(i + 1, 1)

        @block.gpsimd
        def _(pool):
            for q in range(2):
                pool.memset(z[q][:], 0.0).then_inc(zeroed, 1)
            with pool.Fori(0, NB // 2) as i:
                for s in range(2):
                    for g in range(BG):
                        q, gs, r = g % 2, bass.ds(number(i, s, g), 1), turn(i, s, g)
                        ai = tab.pi[:, gs, :].squeeze(1)
                        pool.wait_ge(terms_used[q], r + 1)
                        pool.tensor_tensor(t2p[q][:], tab.b2[:, gs, :].broadcast_to([P, L, CH]),
                                           tab.back_i[:, gs, :].squeeze(1).unsqueeze(2).broadcast_to([P, L, CH]), ALU.mult) \
                            .then_inc(pool_terms[q], 1)
                        pool.tensor_tensor(t2o[q][:], tab.c2[:, gs, :].broadcast_to([P, L + 1, CH]),
                                           ai.unsqueeze(2).broadcast_to([P, L + 1, CH]), ALU.mult) \
                            .then_inc(pool_terms[q], 1)

        @block.vector
        def _(dve):
            for q in range(2):
                dve.sem_inc(terms_used[q], 1)
            dve.sem_inc(p_out, 1)
            dve.sem_inc(r_out, 1)
            dve.wait_ge(zeroed, 2)
            Chain(dve, vstep)(dve.memset(sx[:, :, 0:1], 0.0))

            def table_p(i, s, g):
                q, n, r = g % 2, number(i, s, g), turn(i, s, g)
                gs = bass.ds(n, 1)
                c = Chain(dve, vstep, 1 + 3 * n)
                c(dve.tensor_tensor(pt[q][:], tab.b1[:, gs, :].broadcast_to([P, L, CH]),
                                    tab.back_r[:, gs, :].squeeze(1).unsqueeze(2).broadcast_to([P, L, CH]), ALU.mult))
                c(dve.tensor_single_scalar(z[q][:, SB - 1, :], tab.b1[:, gs, :].squeeze(1), 1.0, ALU.mult))
                dve.wait_ge(pool_terms[q], 2 * r + 1)
                c(dve.tensor_tensor(pt[q][:], pt[q][:], t2p[q][:], ALU.add))
                dve.sem_inc(tabs[q], 1)

            def table_o(i, s, g):
                q, n, r = g % 2, number(i, s, g), turn(i, s, g)
                gs = bass.ds(n, 1)
                c = Chain(dve, ostep, 2 * n)
                c(dve.tensor_tensor(O[s][g][:], tab.c1[:, gs, :].broadcast_to([P, L + 1, CH]),
                                    tab.pr[:, gs, :].squeeze(1).unsqueeze(2).broadcast_to([P, L + 1, CH]), ALU.mult))
                dve.wait_ge(pool_terms[q], 2 * r + 2)
                c(dve.tensor_tensor(O[s][g][:], O[s][g][:], t2o[q][:], ALU.add))
                dve.sem_inc(terms_used[q], 1)
                dve.sem_inc(tab_o, 1)

            def out_p(i, s, g):
                dve.wait_ge(p_psum, number(i, s, g) + 1)
                dve.tensor_copy(pw[g % 2][:], pP[:]).then_inc(p_out, 1)

            def out_r(i, s, g):
                n = number(i, s, g)
                dve.wait_ge(r_psum, n + 1)
                r = flat(R[s][g][:])
                dve.scalar_tensor_tensor(out=r[:, 0:P], in0=ident[:], scalar=tab.skip[:, bass.ds(n, 1)],
                                         in1=flat(pR[:])[:, 0:P], op0=ALU.mult, op1=ALU.add)
                dve.tensor_copy(r[:, P:], flat(pR[:])[:, P:]).then_inc(r_out, 1)

            def matrices(i, s, g):
                n = number(i, s, g)
                dve.wait_ge(diags, LEVELS * n + LEVELS)
                for k in range(LEVELS):
                    m = M[s][:, g, k, :]
                    last = dve.scalar_tensor_tensor(out=m, in0=tab.swap[:], scalar=tab.hb[:, bass.ds(n, 1), k],
                                                    in1=m, op0=ALU.mult, op1=ALU.add)
                last.then_inc(mats, 1)

            def prepare(i, s, wait):
                table_p(i, s, 0)
                table_p(i, s, 1)
                if wait is not None:
                    dve.wait_ge(batch_done, wait)
                table_o(i, s, 0)
                out_p(i, s, 0)
                for g in range(BG):
                    if g + 1 < BG:
                        table_o(i, s, g + 1)
                        out_p(i, s, g + 1)
                    out_r(i, s, g)
                    if g + 2 < BG:
                        table_p(i, s, g + 2)
                    matrices(i, s, g)

            prepare(0, 0, None)

            def body(i, first, last):
                for s in range(2):
                    if not (last and s == 1):
                        ii, ss = at(i, s, 1)
                        prepare(ii, ss, 2 * ii + ss)
            pairs(dve, NB // 2, body)

        @block.scalar
        def _(act):
            act.sem_inc(ut_out, 1)
            act.sem_inc(y_out, 2)
            act.sem_inc(y_st, 16)

            def prepare(i, s, g):
                n = number(i, s, g)
                act.wait_ge(ut_psum, n + 3)
                act.activation(uT[s][g][:], pU[:], ACT.Copy).then_inc(ut_out, 1)
                for k in range(LEVELS):
                    act.activation(M[s][:, g, k, :], ident[:], ACT.Copy, scale=tab.ha[:, bass.ds(n, 1), k]) \
                       .then_inc(diags, 1)

            def copy(i, s, k):
                b = 2 * i + s
                if k == 0:
                    act.wait_ge(v_psum, b + 1)
                    act.wait_ge(level, LEVELS * b + 1)
                else:
                    act.wait_ge(level, LEVELS * b + k + 1)
                act.activation(sc[:], pV[s][:], ACT.Copy).then_inc(copied, 1)

            def before(i, s):
                b = 2 * i + s
                act.wait_ge(level, LEVELS * b + LEVELS + 1)
                act.wait_ge(batch_done, b + 1)
                act.activation(sx[:, :, 1:P], pV[s][:, :, 0:P - 1], ACT.Copy).then_inc(copied, 1)

            def gelu(i, s):
                if s == 0:
                    act.wait_ge(y_st, 16 * i + 16)
                for g in range(BG):
                    act.wait_ge(y_psum, number(i, s, g) + 1)
                    q = (s * BG + g) * CH
                    act.activation(stage[:, :, q:q + CH], pY[g % 2][:], ACT.Gelu_apprx_tanh).then_inc(y_out, 1)
                if s == 1:
                    act.wait_ge(y_out, 2 * BG * i + 2 * BG + 2)
                    act.dma_start(y_view[bass.ds(i, 1)].squeeze(0), stage[:]).then_inc(y_st, 16)

            for g in range(BG):
                prepare(0, 0, g)

            def body(i, first, last):
                for s in range(2):
                    if not (last and s == 1):
                        ii, ss = at(i, s, 1)
                        act.wait_ge(batch_done, 2 * ii + ss)
                    for k in range(LEVELS):
                        copy(i, s, k)
                        if k < BG and not (last and s == 1):
                            prepare(ii, ss, k)
                    before(i, s)
                    gelu(i, s)
            pairs(act, NB // 2, body)
            act.wait_ge(y_st, 16 * (NB // 2) + 16)

        @block.tensor
        def _(pe):
            pe.sem_inc(ut_psum, 2)
            pe.sem_inc(batch_done, 1)
            pe.sem_inc(level, 1)

            def turned(i, s, g):
                n, q, r = number(i, s, g), g % 2, turn(i, s, g)
                pe.wait_ge(u_ld[q], 16 * r + 16)
                pe.wait_ge(ut_out, n + 1)
                for k in range(KB):
                    last = pe.transpose(pU[:, k, :], us[q][:, k, :], ident[:])
                last.then_inc(ut_psum, 1)
                pe.wait_ge(tabs[q], r + 1)
                pe.wait_ge(p_out, n + 1)
                for k in range(KB):
                    last = pe.transpose(pP[:, k, :], flat(pt[q][:])[:, k * P:(k + 1) * P], ident[:])
                last.then_inc(p_psum, 1)

            def inner(i, s, g):
                n, q = number(i, s, g), g % 2
                pe.wait_ge(ut_out, n + 2)
                pe.wait_ge(p_out, n + 2)
                for k in range(KB):
                    last = pe.matmul(pV[s][:, g, :], pw[q][:, k, :], uT[s][g][:, k, :],
                                     start=(g == 0 and k == 0), stop=False, skip_group_check=True)
                if g == BG - 1:
                    last.then_inc(v_psum, 1)
                pe.wait_ge(r_out, n + 1)
                pe.wait_ge(tab_o, n + 1)
                o, r = flat(O[s][g][:]), flat(pR[:])
                for j in range(SB):
                    pe.matmul(r[:, j * CH:P], flat(z[q][:])[:, (SB - 1 - j) * CH:(SB - 1 - j) * CH + P],
                              o[:, 0:(SB - j) * CH], start=j == 0, stop=False, skip_group_check=True)
                pe.matmul(r[:, P:], flat(pt[q][:])[:, (KB - 1) * P:], o[:, CH:CH + (KB - 1) * P],
                          start=False, stop=True, skip_group_check=True).then_inc(r_psum, 1)

            def scan(i, s, k):
                b = 2 * i + s
                if k == 0:
                    pe.wait_ge(mats, BG * b + BG)
                pe.wait_ge(copied, (LEVELS + 1) * b + k + 1)
                h = 1 << k
                for g in range(BG):
                    last = pe.matmul(pV[s][:, g, h:], M[s][:, g, k, :], sc[:, g, 0:P - h], start=False,
                                     stop=(k == LEVELS - 1 and g == BG - 1), skip_group_check=True)
                last.then_inc(level, 1)

            def inside(i, s, g):
                n = number(i, s, g)
                pe.wait_ge(y_out, n + 1)
                pe.wait_ge(r_out, n + 2)
                y, r = flat(pY[g % 2][:]), flat(R[s][g][:])
                for k in range(KB):
                    pe.matmul(y[:, k * P:], uT[s][g][:, k, :], r[:, 0:(KB - k) * P],
                              start=k == 0, stop=False, skip_group_check=True)

            def carry(i, s, g):
                if g == 0:
                    pe.wait_ge(copied, (LEVELS + 1) * (2 * i + s + 1))
                pe.matmul(flat(pY[g % 2][:]), sx[:, g, :], flat(O[s][g][:])[:, CH:], start=False, stop=True,
                          skip_group_check=True).then_inc(y_psum, 1)

            for g in range(BG + 1):
                if g < BG:
                    turned(0, 0, g)
                if g > 0:
                    inner(0, 0, g - 1)

            def body(i, first, last):
                for s in range(2):
                    more = not (last and s == 1)
                    ii, ss = at(i, s, 1)
                    for k in range(LEVELS):
                        if more and k < BG:
                            turned(ii, ss, k)
                        if more and 0 < k <= BG:
                            inner(ii, ss, k - 1)
                        if k >= LEVELS - 2:
                            inside(i, s, k - LEVELS + 2)
                        scan(i, s, k)
                    carry(i, s, 0)
                    carry(i, s, 1)
                    for g in range(2, BG):
                        inside(i, s, g)
                        carry(i, s, g)
                    b = 2 * i + s
                    pe.wait_ge(y_psum, BG * b + BG)
                    pe.sem_inc(batch_done, 1)
            pairs(pe, NB // 2, body)


class SsmTables:

    def __init__(self, core, ctx):
        self.pr, self.pi = core.sbs(ctx, "pow", 2, [P, G, L + 1])
        self.back_r, self.back_i = core.sbs(ctx, "pow_back", 2, [P, G, L])
        self.ha, self.hb = core.sbs(ctx, "pow_high", 2, [P, G, LEVELS])
        self.b1, self.b2, self.c1, self.c2 = core.sbs(ctx, "bc", 4, [P, G, CH])
        self.skip = core.sb(ctx, "skip", [P, G])
        self.swap = core.sb(ctx, "swap", [P, P])



NL = NG + NE


def project(core, ident, tag, layer, glu, src, w, x_view, norm_g, wg, bg, we, be, mod_dram, x1_dram, hn_dram, logits):
    nc = core.nc
    sem = lambda name, n=None: core.sem(f"{tag}_{name}", n)
    NB_ = (4 if glu else 2)
    const_ld, w_ld, s_ld, x_ld = sem("const_loaded"), sem("w_loaded", KD), sem("src_loaded", 2), sem("x_loaded", 2)
    w_hi_ready, w_split, step = sem("w_hi"), sem("w_split"), sem("dve_step")
    tp, thi, tlo, mm = sem("transposed", 2), sem("hi", 2), sem("lo", 2), sem("bank")
    gated, out_read = sem("gate"), sem("product_read")
    x1_ready, x1_st, hn_st = sem("x1_ready", 2), sem("x1_stored", 2), sem("hn_stored", 2)
    var, std, hn_ready = sem("var"), sem("std"), sem("hn_ready", 2)
    ht_psum, ht_out, lg_psum, lg_out = sem("hT_in_psum"), sem("hT_out"), sem("logits_in_psum"), sem("logits_out")
    with ExitStack() as ctx:
        sb = lambda name, shape, dt=F32: core.sb(ctx, f"{tag}_{name}", shape, dt)
        sbs = lambda name, n, shape, dt=F32: core.sbs(ctx, f"{tag}_{name}", n, shape, dt)
        cols = NB_ * HALF
        w_raw, w_lo = core.raw_low(ctx, f"{tag}_w", [P, KD, cols])
        w_hi = sb("w_hi", [P, KD, cols], F32R)
        gate1, gain, shift = sb("gate1", [P, D]), sb("gain", [P, D]), sb("shift", [P, D])
        wr, br = sb("router", [P, KD, NL]), sb("router_bias", [P, NL])
        srcb = sbs("src", 2, [P, KD, P])
        xb, hn = sbs("x", 2, [P, D]), sbs("hn", 2, [P, D])
        h_hi, h_lo = sbs("sT_hi", 2, [P, KD, P], F32R), sbs("sT_lo", 2, [P, KD, P], F32R)
        acc = sb("acc", [P, 2, HALF])
        hT = sb("hT", [P, KD, P])
        stat = sbs("stat", 2, [P, 4])
        pT = core.ps(ctx, f"{tag}_pT", [P, KD, P]) if glu else None
        pM = [core.ps(ctx, f"{tag}_pM{s}", [P, NB_, HALF]) for s in range(1 if glu else 2)] * (2 if glu else 1)
        pH = core.ps(ctx, f"{tag}_pH", [P, KD, P])
        accf = acc[:].rearrange("p a b -> p (a b)")
        block = ctx.enter_context(nc.Block())
        order = (2, 3, 0, 1) if glu else (0, 1)
        if glu:
            src_view = src.rearrange("(n p) (k f) -> n p k f", p=P, f=P)
        else:
            src_view = src.rearrange("(k p) (n f) -> n p k f", p=P, f=P)
        x1_view = x1_dram.rearrange("(n p) d -> n p d", p=P)
        hn_view = hn_dram.rearrange("(n p) d -> n p d", p=P)
        tile_of = lambda view, i, s: view[bass.ds(2 * i + s, 1)].squeeze(0)

        @block.sync
        def _(sp):
            def load_src(i, s):
                sp.wait_ge(tlo[s], i + 1)
                sp.dma_start(srcb[s][:], tile_of(src_view, i, s)).then_inc(s_ld[s], 16)

            def load_x(i, s):
                sp.dma_start(xb[s][:], tile_of(x_view, i, s)).then_inc(x_ld[s], 16)

            def store(i, s):
                sp.wait_ge(x1_ready[s], i + 1)
                sp.dma_start(tile_of(x1_view, i, s), xb[s][:]).then_inc(x1_st[s], 16)
                sp.wait_ge(hn_ready[s], i + 1)
                sp.dma_start(tile_of(hn_view, i, s), hn[s][:]).then_inc(hn_st[s], 16)

            sp.dma_start(gate1[:], row(mod_dram[layer:layer + 1, :], G1 * D, D)).then_inc(const_ld, 16)
            sp.dma_start(gain[:], row(norm_g[layer:layer + 1, :], 0, D)).then_inc(const_ld, 16)
            load_mod(sp, mod_dram, layer, SC2, hn[0][:], const_ld)
            load_mod(sp, mod_dram, layer, SH2, shift[:], const_ld)
            sp.dma_start(wr[:, :, 0:NG], wg[layer].rearrange("(k p) n -> p k n", p=P)).then_inc(const_ld, 16)
            sp.dma_start(wr[:, :, NG:], we[layer].rearrange("(k p) n -> p k n", p=P)).then_inc(const_ld, 16)
            sp.dma_start(br[:, 0:NG], row(bg[layer:layer + 1, :], 0, NG)).then_inc(const_ld, 16)
            sp.dma_start(br[:, NG:], row(be[layer:layer + 1, :], 0, NE)).then_inc(const_ld, 16)
            load_src(0, 0)
            load_src(0, 1)
            for k in range(KD):
                sp.dma_start(w_raw[:, k, :], w.rearrange("(k p) n -> k p n", p=P)[k]).then_inc(w_ld[k], 16)
            load_x(0, 0)
            load_x(0, 1)
            with sp.Fori(0, NT // 2 - 1) as i:
                for s in range(2):
                    load_src(i + 1, s)
                    store(i, s)
                    sp.wait_ge(x1_st[s], 16 * i + 16)
                    load_x(i + 1, s)
            for s in range(2):
                store(NT // 2 - 1, s)
            for s in range(2):
                sp.wait_ge(x1_st[s], 16 * (NT // 2))
                sp.wait_ge(hn_st[s], 16 * (NT // 2))

        @block.vector
        def _(dve):
            dve.wait_ge(const_ld, 8 * 16)
            base = 2
            c = Chain(dve, step)
            fold_scale(dve, c, gain[:], hn[0][:])
            c(dve.tensor_scalar(gate1[:], gate1[:], 1.0, None, ALU.add))

            def low(i, s):
                dve.wait_ge(thi[s], 2 * i + 2)
                raw = pT if glu else srcb[s]
                dve.tensor_tensor(h_lo[s][:], raw[:], h_hi[s][:].bitcast(F32), ALU.subtract).then_inc(tlo[s], 1)

            def finish(i, s):
                n = 2 * i + s
                c = Chain(dve, step, base + (6 if glu else 5) * n)
                dve.wait_ge(mm, NB_ * n + NB_)
                dve.wait_ge(x_ld[s], 16 * i + 16)
                if glu:
                    dve.wait_ge(gated, 2 * n + 2)
                    c(dve.tensor_tensor(acc[:], pM[s][:, 0:2, :], acc[:], ALU.mult))
                    dve.sem_inc(out_read, 1)
                    c(dve.tensor_tensor(accf, accf, gate1[:], ALU.mult))
                else:
                    c(dve.tensor_tensor(accf, pM[s][:].rearrange("p a b -> p (a b)"), gate1[:], ALU.mult))
                    dve.sem_inc(out_read, 1)
                c(dve.tensor_tensor(xb[s][:], accf, xb[s][:], ALU.add))
                dve.sem_inc(x1_ready[s], 1)
                c(dve.tensor_tensor_reduce(out=accf, in0=xb[s][:], in1=xb[s][:], scale=1.0, scalar=0.0,
                                           op0=ALU.mult, op1=ALU.add, accum_out=stat[s][:, 0:1]))
                dve.tensor_scalar(stat[s][:, 1:2], stat[s][:, 0:1], 1.0 / D, EPS, ALU.mult, ALU.add).then_inc(var, 1)
                dve.wait_ge(std, n + 1)
                c(dve.reciprocal(stat[s][:, 3:4], stat[s][:, 2:3]))
                if not (isinstance(i, int) and i == 0):
                    dve.wait_ge(hn_st[s], 16 * i)
                    dve.wait_ge(ht_psum, n)
                c(dve.scalar_tensor_tensor(out=hn[s][:], in0=xb[s][:], scalar=stat[s][:, 3:4], in1=gain[:],
                                           op0=ALU.mult, op1=ALU.mult))
                dve.tensor_tensor(hn[s][:], hn[s][:], shift[:], ALU.add).then_inc(hn_ready[s], 1)

            def out_logits(i, s):
                n = 2 * i + s
                dve.wait_ge(lg_psum, n + 1)
                dve.tensor_tensor(logits[:, bass.ds(n, 1), :].squeeze(1), pH[:, 0, 0:NL], br[:], ALU.add) \
                   .then_inc(lg_out, 1)

            low(0, 0)
            for k in range(KD):
                dve.wait_ge(w_hi_ready, k + 1)
                dve.tensor_tensor(w_lo[:, k, :], w_raw[:, k, :], w_hi[:, k, :].bitcast(F32), ALU.subtract) \
                   .then_inc(w_split, 1)

            def body(i, first, last):
                for s in range(2):
                    if not (last and s == 1):
                        low(*at(i, s, 1))
                    if not first:
                        out_logits(*at(i, s, -2))
                    finish(i, s)
            pairs(dve, NT // 2, body)
            out_logits(NT // 2 - 1, 0)
            out_logits(NT // 2 - 1, 1)

        @block.scalar
        def _(act):
            act.sem_inc(ht_out, 1)
            for s in range(2):
                act.sem_inc(tlo[s], 1)

            def high(i, s):
                if glu:
                    act.wait_ge(tp[s], i + 1)
                else:
                    act.wait_ge(s_ld[s], 16 * i + 16)
                if not (isinstance(i, int) and i == 0):
                    act.wait_ge(mm, NB_ * (2 * i + s) - NB_)
                raw = pT if glu else srcb[s]
                for h in range(2):
                    act.activation(h_hi[s][:, 4 * h:4 * h + 4, :], raw[:, 4 * h:4 * h + 4, :], ACT.Copy) \
                       .then_inc(thi[s], 1)

            def gate(i, s):
                n = 2 * i + s
                act.wait_ge(var, n + 1)
                for h in range(2):
                    act.wait_ge(mm, NB_ * n + h + 1)
                    act.activation(acc[:, h, :], pM[s][:, 2 + h, :], ACT.Sigmoid).then_inc(gated, 1)

            def std_of(i, s):
                n = 2 * i + s
                act.wait_ge(var, n + (2 if glu else 1))
                act.activation(stat[s][:, 2:3], stat[s][:, 1:2], ACT.Sqrt).then_inc(std, 1)

            def out_h(i, s):
                n = 2 * i + s
                act.wait_ge(ht_psum, n + 2)
                act.activation(hT[:], pH[:], ACT.Copy).then_inc(ht_out, 1)

            if glu:
                act.sem_inc(var, 1)
            high(0, 0)
            for k in range(KD):
                act.wait_ge(w_ld[k], 16)
                act.activation(w_hi[:, k, :], w_raw[:, k, :], ACT.Copy).then_inc(w_hi_ready, 1)

            def body(i, first, last):
                for s in range(2):
                    if not (last and s == 1):
                        high(*at(i, s, 1))
                    if glu:
                        gate(i, s)
                    if not (first and s == 0):
                        out_h(*at(i, s, -1))
                    std_of(i, s)
            pairs(act, NT // 2, body)
            out_h(NT // 2 - 1, 1)

        @block.tensor
        def _(pe):
            pe.sem_inc(ht_psum, 1)
            pe.sem_inc(out_read, 1 if glu else 2)

            def turned(i, s):
                pe.wait_ge(s_ld[s], 16 * i + 16)
                pe.wait_ge(tlo[(s + 1) % 2], i + 1 + (0 if s == 0 else 1))
                for k in range(KD):
                    last = pe.transpose(pT[:, k, :], srcb[s][:, k, :], ident[:])
                last.then_inc(tp[s], 1)

            def products(i, s):
                n = 2 * i + s
                pe.wait_ge(tlo[s], i + 2)
                if not glu:
                    pe.wait_ge(out_read, n + 1)
                elif not (isinstance(n, int) and n == 0):
                    pe.wait_ge(gated, 2 * n)
                for b in order:
                    if glu and b == 0:
                        pe.wait_ge(out_read, n + 1)
                    for k in range(KD):
                        if b == order[0] and isinstance(i, int) and i + s == 0:
                            pe.wait_ge(w_split, k + 1)
                        last = product(pe, pM[s][:, b, :], (h_hi[s][:, k, :], h_lo[s][:, k, :]),
                                       (w_hi[:, k, bass.ts(b, HALF)], w_lo[:, k, bass.ts(b, HALF)]),
                                       k == 0, k == KD - 1)
                    last.then_inc(mm, 1)

            def turned_hn(i, s):
                n = 2 * i + s
                pe.wait_ge(hn_ready[s], i + 1)
                if not (isinstance(n, int) and n == 0):
                    pe.wait_ge(lg_out, n)
                for k in range(KD):
                    last = pe.transpose(pH[:, k, :], hn[s][:, k * P:(k + 1) * P], ident[:])
                last.then_inc(ht_psum, 1)

            def router(i, s):
                n = 2 * i + s
                pe.wait_ge(ht_out, n + 2)
                for k in range(KD):
                    last = pe.matmul(pH[:, 0, 0:NL], hT[:, k, :], wr[:, k, :], start=k == 0, stop=k == KD - 1)
                last.then_inc(lg_psum, 1)

            if glu:
                turned(0, 0)

            def body(i, first, last):
                for s in range(2):
                    if glu and not (last and s == 1):
                        turned(*at(i, s, 1))
                    if not first:
                        router(*at(i, s, -2))
                    products(i, s)
                    if not (first and s == 0):
                        turned_hn(*at(i, s, -1))
            pairs(pe, NT // 2, body)
            router(NT // 2 - 1, 0)
            turned_hn(NT // 2 - 1, 1)
            router(NT // 2 - 1, 1)



def routing(core, tag, logits, pos, wts, table, slot_dram, *mod_args):
    nc = core.nc
    sem = lambda name: core.sem(f"{tag}_{name}")
    step, istep, to_act, to_dve = sem("dve_step"), sem("pool_step"), sem("for_act"), sem("from_act")
    mask_ready, counted, zero_st, pos_ready, sc_st = sem("mask"), sem("counted"), sem("zeroed"), sem("pos_ready"), sem("scattered")
    with ExitStack() as ctx:
        sb = lambda name, shape, dt=F32: core.sb(ctx, f"{tag}_{name}", shape, dt)
        upper, ones = sb("upper", [P, P]), sb("ones", [P, P])
        io_i, io = sb("iota_i", [P, EG], I32), sb("iota", [P, EG])
        tok = sb("token", [P, NT], I32)
        zt = sb("zeros", [P, TILES + 1], I32)
        a1, a2, a3 = sb("t1", [P, NT, 1]), sb("t2", [P, NT, 1]), sb("t3", [P, NT, 1])
        m1, m2, gp = sb("m1", [P, NT, 1]), sb("m2", [P, NT, 1]), sb("gp", [P, NT, 1])
        g4, ohg = sb("g4", [P, NT, NG]), sb("ohg", [P, NT, NG])
        es, tmp = sb("e_sel", [P, NT, EG]), sb("tmp", [P, NT, EG])
        ohk = [sb(f"ohk{k}", [P, NT, EG]) for k in range(2)]
        OH = [sb(f"oh{k}", [P, NT, NE]) for k in range(2)]
        M, C0, C1_, V = (sb(n, [P, NT, NE]) for n in ("mask", "c0", "c1", "v"))
        ti, tf, tg = sb("tiles_i", [P, NE], I32), sb("tiles", [P, NE]), sb("tiles2", [P, NE])
        own = sb("own", [P, NE])
        posf = sb("posf", [P, NT, 2])
        pr = core.ps(ctx, f"{tag}_rank", [P, NT * NE])
        pc = core.ps(ctx, f"{tag}_count", [P, NT * NE])
        mod = Modulation(core, ctx, *mod_args) if mod_args else None
        block = ctx.enter_context(nc.Block())
        flat = lambda a: a.rearrange("p a b -> p (a b)")

        @block.gpsimd
        def _(pool):
            c = Chain(pool, istep)
            c(pool.memset(ones[:], 1.0))
            c(pool.affine_select(out=upper[:], in_=ones[:], compare_op=ALU.is_gt, fill=0.0, base=0,
                                 pattern=[[1, P]], channel_multiplier=-1))
            c(pool.iota(io_i[:], pattern=[[1, EG]], base=-EG, channel_multiplier=0))
            c(pool.iota(tok[:], pattern=[[P, NT]], base=0, channel_multiplier=1))
            c(pool.memset(zt[:], 0))
            pool.dma_start(slot_dram.rearrange("(p n) one -> p (n one)", p=P), zt[:]).then_inc(zero_st, 16)
            pool.wait_ge(zero_st, 16)
            for k in range(2):
                pool.wait_ge(pos_ready, k + 1)
                for t in range(NT):
                    pool.indirect_dma_start(slot_dram, bass.IndirectOffsetOnAxis(ap=pos[:, t, k:k + 1], axis=0),
                                            tok[:, t:t + 1], None).then_inc(sc_st, 16)
            pool.wait_ge(sc_st, 16 * 2 * NT)

        @block.scalar
        def _(act):
            if mod:
                mod.cond(act)
            act.wait_ge(to_act, 1)
            act.activation(g4[:], g4[:], ACT.Exp).then_inc(to_dve, 1)
            act.wait_ge(to_act, 2)
            act.activation(a3[:], a3[:], ACT.Exp).then_inc(to_dve, 1)
            if mod:
                mod.results(act)

        @block.tensor
        def _(pe):
            if mod:
                mod.start(pe)
                mod.products(pe, 0, 1)
            pe.wait_ge(mask_ready, 1)
            for lhs, out in ((upper, pr), (ones, pc)):
                for h in range(2):
                    last = pe.matmul(out[:, h * HALF:(h + 1) * HALF], lhs[:], flat(M[:])[:, h * HALF:(h + 1) * HALF],
                                     start=True, stop=True)
            last.then_inc(counted, 1)
            if mod:
                mod.products(pe, 1, mod.ROUNDS)

        if mod:
            @block.sync
            def _(sp):
                mod.first_loads(sp)
                mod.loads(sp)
                mod.store(sp)

        @block.vector
        def _(dve):
            c = Chain(dve, step)
            tt, ts, red, copy = dve.tensor_tensor, dve.tensor_scalar, dve.tensor_reduce, dve.tensor_copy
            bc = lambda a, n: a.broadcast_to([P, NT, n])

            def first_of(values, best, n, out):
                t_ = tmp[:, :, 0:n]
                c(tt(t_, values, bc(best, n), ALU.is_equal))
                c(tt(t_, t_, io[:, 0:n].unsqueeze(1).broadcast_to([P, NT, n]), ALU.mult))
                c(red(a2[:], t_, AX.X, ALU.min))
                c(tt(out, io[:, 0:n].unsqueeze(1).broadcast_to([P, NT, n]), bc(a2[:], n), ALU.is_equal))

            dve.wait_ge(istep, 5)
            c(copy(io[:], io_i[:]))
            gl = logits[:, :, 0:NG]
            c(red(m1[:], gl, AX.X, ALU.max))
            c(tt(g4[:], gl, bc(m1[:], NG), ALU.subtract))
            dve.sem_inc(to_act, 1)
            first_of(gl, m1[:], NG, ohg[:])
            dve.wait_ge(to_dve, 1)
            c(red(a1[:], g4[:], AX.X, ALU.add))
            c(dve.reciprocal(gp[:], a1[:]))
            for g in range(NG):
                el = logits[:, :, NG + g * EG:NG + (g + 1) * EG]
                dst = es if g == 0 else tmp
                c(tt(dst[:], el, bc(ohg[:, :, g:g + 1], EG), ALU.mult))
                if g:
                    c(tt(es[:], es[:], tmp[:], ALU.add))
            c(red(m1[:], es[:], AX.X, ALU.max))
            first_of(es[:], m1[:], EG, ohk[0][:])
            c(dve.scalar_tensor_tensor(out=es[:], in0=ohk[0][:], scalar=-3.0e38, in1=es[:], op0=ALU.mult, op1=ALU.add))
            c(red(m2[:], es[:], AX.X, ALU.max))
            first_of(es[:], m2[:], EG, ohk[1][:])
            c(tt(a3[:], m2[:], m1[:], ALU.subtract))
            dve.sem_inc(to_act, 1)
            dve.wait_ge(to_dve, 2)
            c(ts(a1[:], a3[:], 1.0, None, ALU.add))
            c(dve.reciprocal(a1[:], a1[:]))
            c(tt(a1[:], a1[:], gp[:], ALU.mult))
            c(copy(wts[:, :, 0:1], a1[:]))
            c(tt(wts[:, :, 1:2], a1[:], a3[:], ALU.mult))
            for k in range(2):
                c(tt(OH[k][:].rearrange("p t (g e) -> p t g e", g=NG),
                     ohg[:].unsqueeze(3).broadcast_to([P, NT, NG, EG]),
                     ohk[k][:].unsqueeze(2).broadcast_to([P, NT, NG, EG]), ALU.mult))
            c(tt(M[:], OH[0][:], OH[1][:], ALU.add))
            dve.sem_inc(mask_ready, 1)
            dve.wait_ge(counted, 1)
            src, dst = C0, C1_
            c(copy(flat(src[:]), pc[:]))
            h = 1
            while h < NT:
                c(copy(dst[:, 0:h, :], src[:, 0:h, :]))
                c(tt(dst[:, h:, :], src[:, h:, :], src[:, 0:NT - h, :], ALU.add))
                src, dst = dst, src
                h *= 2
            c(ts(tf[:], src[:, NT - 1, :], float(P - 1), None, ALU.add))
            c(copy(ti[:], tf[:]))
            c(dve.tensor_single_scalar(ti[:], ti[:], 7, ALU.arith_shift_right))
            c(copy(own[:], ti[:]))
            c(ts(own[:], own[:], 1.0, None, ALU.max))
            c(copy(tf[:], own[:]))
            x, y = tf, tg
            h = 1
            while h < NE:
                c(copy(y[:, 0:h], x[:, 0:h]))
                c(tt(y[:, h:], x[:, h:], x[:, 0:NE - h], ALU.add))
                x, y = y, x
                h *= 2
            c(copy(table[:, 2 * NE:], x[0:1, NE - 1:NE]))
            c(tt(x[:], x[:], own[:], ALU.subtract))
            c(copy(table[:, 0:NE], x[0:1, :]))
            c(ts(own[:], own[:], -1.0, None, ALU.add))
            c(copy(table[:, NE:2 * NE], own[0:1, :]))
            c(ts(x[:], x[:], float(P), None, ALU.mult))
            c(tt(flat(V[:]), flat(src[:]), pc[:], ALU.subtract))
            c(tt(flat(V[:]), flat(V[:]), pr[:], ALU.add))
            c(tt(V[:], V[:], x[:].unsqueeze(1).broadcast_to([P, NT, NE]), ALU.add))
            for k in range(2):
                c(tt(OH[k][:], OH[k][:], V[:], ALU.mult))
                c(red(posf[:, :, k:k + 1], OH[k][:], AX.X, ALU.add))
                c(copy(pos[:, :, k:k + 1], posf[:, :, k:k + 1]))
                dve.sem_inc(pos_ready, 1)
            if mod:
                mod.biases(dve)



def experts(core, ident, tag, layer, w1, w3, w2, mod_dram, table, slot_dram, hn_dram, o_dram):
    nc = core.nc
    sem = lambda name, n=None: core.sem(f"{tag}_{name}", n)
    CQ = KD // 2
    w13_ld, w13_hi, w13_lo = [sem(f"w13_loaded{s}_", CQ) for s in range(2)], sem("w13_hi"), sem("w13_lo")
    w2_ld, w2_hi, w2_lo = sem("w2_loaded", 2), sem("w2_hi"), sem("w2_lo")
    gate_ld, gate_ready = sem("gate_loaded"), sem("gate_ready")
    ix_ld, x_ld, gath = sem("idx_loaded"), sem("rows_loaded"), sem("gathers")
    xt_psum, xt_hi, xt_lo, ab, hh = sem("xT_in_psum"), sem("xT_hi"), sem("xT_lo"), sem("ab_in_psum"), sem("h_ready")
    sil, ht_psum, ht_hi, ht_lo = sem("silu"), sem("hT_in_psum"), sem("hT_hi"), sem("hT_lo")
    o_psum, o_out, o_st = sem("o_in_psum"), sem("o_out"), sem("o_stored")
    stored_all, zeroed, z_st = sem("all_stored"), sem("zeroed"), sem("zeros_stored")
    with ExitStack() as ctx:
        sb = lambda name, shape, dt=F32: core.sb(ctx, f"{tag}_{name}", shape, dt)
        split = lambda name, shape: core.raw_low(ctx, f"{tag}_{name}", shape) + (sb(name + "_hi", shape, F32R),)
        W13 = [split(f"w13_{s}", [P, 2, KD, FE]) for s in range(2)]
        W2 = split("w2", [P, 2, KF, HALF])
        gate2 = sb("gate2", [P, 2, HALF])
        ix, xg = sb("idx", [P, 1], I32), sb("rows", [P, D])
        xT_hi, xT_lo = sb("xT_hi", [P, KD, P], F32R), sb("xT_lo", [P, KD, P], F32R)
        h = sb("h", [P, FE])
        hT_hi, hT_lo = sb("hT_hi", [P, KF, P], F32R), sb("hT_lo", [P, KF, P], F32R)
        ob, zeros = sb("o", [P, 2, HALF]), sb("zeros", [P, D])
        pX = core.ps(ctx, f"{tag}_pX", [P, KD, P])
        pA, pB = (core.ps(ctx, f"{tag}_{n}", [P, HALF]) for n in ("pA", "pB"))
        pH = core.ps(ctx, f"{tag}_pH", [P, 2, HALF])
        pO = core.ps(ctx, f"{tag}_pO", [P, 2, HALF])
        block = ctx.enter_context(nc.Block())
        slots = slot_dram.rearrange("(n p) one -> n p one", p=P)
        o_view = o_dram.rearrange("(n p) d -> n p (d)", p=P)
        w13_view = [w[layer].rearrange("e (q k p) n -> e q p k n", k=2, p=P) for w in (w1, w3)]
        w2_view = w2[layer].rearrange("e (k p) (n f) -> e n p k f", p=P, f=HALF)
        of = lambda view, e: view[bass.ds(e, 1)].squeeze(0)

        def span(eng, e):
            return (eng.value_load(table[0:1, bass.ds(e, 1)], min_val=0, max_val=TILES - 1),
                    eng.value_load(table[0:1, bass.ds(e + NE, 1)], min_val=0, max_val=TILES - 1))

        @block.sync
        def _(sp):
            def load_w13(e, s, parts=range(CQ)):
                for q in parts:
                    for m in range(2):
                        sp.dma_start(W13[s][0][:, m, 2 * q:2 * q + 2, :], of(w13_view[m], e)[q]) \
                          .then_inc(w13_ld[s][q], 16)

            def load_w2(e, n):
                sp.dma_start(W2[0][:, n, :, :], of(w2_view, e)[n]).then_inc(w2_ld[n], 16)

            sp.dma_start(gate2[:].rearrange("p a b -> p (a b)"), row(mod_dram[layer:layer + 1, :], G2 * D, D)) \
              .then_inc(gate_ld, 16)
            load_w13(0, 0, (0, 1))
            sp.wait_ge(x_ld, 16)
            load_w13(0, 0, (2, 3))

            def body(i, first, last):
                for s in range(2):
                    e = 2 * i + s
                    if not (first and s == 0):
                        t, _ = span(sp, e)
                        sp.wait_ge(o_psum, 2 * t + 1)
                    load_w2(e, 0)
                    if not (first and s == 0):
                        sp.wait_ge(o_psum, 2 * t + 2)
                    load_w2(e, 1)
                    if not (last and s == 1):
                        load_w13(e + 1, 1 - s)
            pairs(sp, NE // 2, body)
            n = sp.value_load(table[0:1, 2 * NE:2 * NE + 1], min_val=NE, max_val=TILES)
            sp.wait_ge(zeroed, 1)
            with sp.Fori(NE, TILES) as t:
                with sp.If(t >= n):
                    sp.dma_start(of(o_view, t), zeros[:]).then_inc(z_st, 16)
                with sp.Else():
                    sp.sem_inc(z_st, 16)
            sp.wait_ge(z_st, 16 * (TILES - NE))

        @block.gpsimd
        def _(pool):
            pool.memset(zeros[:], 0.0).then_inc(zeroed, 1)
            n = pool.value_load(table[0:1, 2 * NE:2 * NE + 1], min_val=NE, max_val=TILES)
            with pool.Fori(0, n + 1) as t:
                pool.dma_start(ix[:], slots[bass.ds(t, 1)].squeeze(0)).then_inc(ix_ld, 16)
                pool.wait_ge(ix_ld, 16 * t + 16)
                pool.wait_ge(xt_psum, t + 1)
                pool.sem_inc(gath, 1)
                pool.indirect_dma_start(xg[:], None, hn_dram, bass.IndirectOffsetOnAxis(ap=ix[:, 0:1], axis=0)) \
                    .then_inc(x_ld, 16)
                pool.wait_ge(x_ld, 16 * t + 16)

        @block.tensor
        def _(pe):
            pe.sem_inc(xt_psum, 1)
            pe.sem_inc(o_psum, 2)
            pe.sem_inc(ht_psum, 1)

            def turn_x(a, b):
                for k in range(a, b):
                    last = pe.transpose(pX[:, k, :], xg[:, k * P:(k + 1) * P], ident[:])
                return last

            def tile(t, e, s):
                pe.wait_ge(xt_lo, 2 * t + 2)
                pe.wait_ge(hh, 2 * t + 2)
                for m, out in enumerate((pA, pB)):
                    for k in range(KD):
                        if m == 0 and k % 2 == 0:
                            pe.wait_ge(w13_lo, CQ * e + k // 2 + 1)
                        last = product(pe, out[:], (xT_hi[:, k, :], xT_lo[:, k, :]),
                                       (W13[s][2][:, m, k, :], W13[s][1][:, m, k, :]), k == 0, k == KD - 1)
                    last.then_inc(ab, 1)
                pe.wait_ge(x_ld, 16 * t + 32)
                turn_x(0, 4)
                for k in range(KF):
                    if k % 2 == 0:
                        pe.wait_ge(hh, 2 * t + 3 + k // 2)
                    last = pe.transpose(pH[:, k // 2, (k % 2) * P:(k % 2 + 1) * P], h[:, k * P:(k + 1) * P], ident[:])
                last.then_inc(ht_psum, 1)
                turn_x(4, KD).then_inc(xt_psum, 1)
                for n in range(2):
                    pe.wait_ge(w2_lo, 4 * e + 2 * n + 2)
                    pe.wait_ge(o_out, 2 * t + n + 1)
                    for k in range(KF):
                        if n == 0 and k % 2 == 0:
                            pe.wait_ge(ht_hi, 2 * t + k // 2 + 1)
                        for w in (1, 2):
                            pe.matmul(pO[:, n, :], hT_hi[:, k, :], W2[w][:, n, k, :], start=k == 0 and w == 1, stop=False)
                    for k in range(KF):
                        if n == 0 and k % 2 == 0:
                            pe.wait_ge(ht_lo, 2 * t + k // 2 + 1)
                        last = pe.matmul(pO[:, n, :], hT_lo[:, k, :], W2[2][:, n, k, :], start=False, stop=k == KF - 1)
                    last.then_inc(o_psum, 1)

            pe.wait_ge(x_ld, 16)
            turn_x(0, KD).then_inc(xt_psum, 1)
            with pe.Fori(0, NE // 2) as i:
                for s in range(2):
                    e = 2 * i + s
                    t0, rest = span(pe, e)
                    with pe.Fori(0, rest + 1) as j:
                        tile(t0 + j, e, s)

        @block.scalar
        def _(act):
            act.sem_inc(o_st, 16)

            def split_w13(e, s, round_, parts):
                for q in parts:
                    act.wait_ge(w13_ld[s][q], 32 * round_ + 32)
                    act.activation(W13[s][2][:, :, 2 * q:2 * q + 2, :], W13[s][0][:, :, 2 * q:2 * q + 2, :], ACT.Copy) \
                       .then_inc(w13_hi, 1)

            def split_w2(e):
                for n in range(2):
                    act.wait_ge(w2_ld[n], 16 * e + 16)
                    for k in (0, 2):
                        act.activation(W2[2][:, n, k:k + 2, :], W2[0][:, n, k:k + 2, :], ACT.Copy).then_inc(w2_hi, 1)

            def out_x(t):
                act.wait_ge(xt_psum, t + 2)
                for q in range(2):
                    act.activation(xT_hi[:, 4 * q:4 * q + 4, :], pX[:, 4 * q:4 * q + 4, :], ACT.Copy).then_inc(xt_hi, 1)

            def tile(t, late=None):
                act.wait_ge(ab, 2 * t + 1)
                act.wait_ge(ht_psum, t + 1)
                act.activation(h[:], pA[:], ACT.Silu).then_inc(sil, 1)
                act.wait_ge(ht_psum, t + 2)
                for q in range(2):
                    act.activation(hT_hi[:, 2 * q:2 * q + 2, :], pH[:, q, 0:2 * P].rearrange("p (a b) -> p a b", b=P), ACT.Copy).then_inc(ht_hi, 1)
                out_x(t + 1)
                if late is not None:
                    split_w13(*late, range(CQ - 1, CQ))
                act.wait_ge(o_out, 2 * t + 4)
                at_tile = nc.s_assert_within(t, 0, TILES - 1, skip_runtime_bounds_check_because="no choice of experts "
                                          "fills more than TILES tiles")
                act.dma_start(of(o_view, at_tile), ob[:].rearrange("p a b -> p (a b)")).then_inc(o_st, 16)

            out_x(0)
            split_w13(0, 0, 0, range(CQ))

            def body(i, first, last):
                for s in range(2):
                    e = 2 * i + s
                    t0, rest = span(act, e)
                    split_w2(e)
                    with act.If(rest > 0):
                        with act.Fori(0, rest) as j:
                            tile(t0 + j)
                    late = None if last and s == 1 else (e + 1, 1 - s, at(i, s, 1)[0])
                    if late is not None:
                        split_w13(*late, range(CQ - 1))
                    tile(t0 + rest, late)
            pairs(act, NE // 2, body)
            n = act.value_load(table[0:1, 2 * NE:2 * NE + 1], min_val=NE, max_val=TILES)
            act.wait_ge(o_st, 16 * n + 16)
            act.sem_inc(stored_all, 1)

        @block.vector
        def _(dve):
            dve.sem_inc(hh, 2)
            dve.sem_inc(o_out, 2)
            dve.wait_ge(gate_ld, 16)
            dve.tensor_scalar(gate2[:], gate2[:], 1.0, None, ALU.add).then_inc(gate_ready, 1)
            dve.wait_ge(gate_ready, 1)

            def split_w13(e, s, parts):
                for q in parts:
                    dve.wait_ge(w13_hi, CQ * e + q + 1)
                    c = slice(2 * q, 2 * q + 2)
                    dve.tensor_tensor(W13[s][1][:, :, c, :], W13[s][0][:, :, c, :],
                                      W13[s][2][:, :, c, :].bitcast(F32), ALU.subtract).then_inc(w13_lo, 1)

            def split_w2(e):
                for n in range(2):
                    for k in (0, 2):
                        dve.wait_ge(w2_hi, 4 * e + 2 * n + k // 2 + 1)
                        dve.tensor_tensor(W2[1][:, n, k:k + 2, :], W2[0][:, n, k:k + 2, :],
                                          W2[2][:, n, k:k + 2, :].bitcast(F32), ALU.subtract).then_inc(w2_lo, 1)

            def out_x(t):
                for q in range(2):
                    dve.wait_ge(xt_hi, 2 * t + q + 1)
                    dve.tensor_tensor(xT_lo[:, 4 * q:4 * q + 4, :], pX[:, 4 * q:4 * q + 4, :],
                                      xT_hi[:, 4 * q:4 * q + 4, :].bitcast(F32), ALU.subtract).then_inc(xt_lo, 1)

            def tile(t, late=None):
                dve.wait_ge(ab, 2 * t + 2)
                dve.wait_ge(sil, t + 1)
                for q in range(2):
                    c = slice(q * 2 * P, (q + 1) * 2 * P)
                    dve.tensor_tensor(h[:, c], h[:, c], pB[:, c], ALU.mult).then_inc(hh, 1)
                for q in range(2):
                    dve.wait_ge(ht_hi, 2 * t + q + 1)
                    dve.tensor_tensor(hT_lo[:, 2 * q:2 * q + 2, :], pH[:, q, 0:2 * P].rearrange("p (a b) -> p a b", b=P),
                                      hT_hi[:, 2 * q:2 * q + 2, :].bitcast(F32), ALU.subtract).then_inc(ht_lo, 1)
                out_x(t + 1)
                if late is not None:
                    split_w13(*late, range(CQ - 1, CQ))
                for n in range(2):
                    dve.wait_ge(o_psum, 2 * t + n + 3)
                    if n == 0:
                        dve.wait_ge(o_st, 16 * t + 16)
                    dve.tensor_tensor(ob[:, n, :], pO[:, n, :], gate2[:, n, :], ALU.mult).then_inc(o_out, 1)

            out_x(0)
            split_w13(0, 0, range(CQ))

            def body(i, first, last):
                for s in range(2):
                    e = 2 * i + s
                    t0, rest = span(dve, e)
                    split_w2(e)
                    with dve.If(rest > 0):
                        with dve.Fori(0, rest) as j:
                            tile(t0 + j)
                    late = None if last and s == 1 else (e + 1, 1 - s)
                    if late is not None:
                        split_w13(*late, range(CQ - 1))
                    tile(t0 + rest, late)
            pairs(dve, NE // 2, body)



def combine(core, ident, tag, layer, pos, wts, o_dram, x1_dram, mod_dram, gain_src, x2_dram=None, hnT_dram=None,
            out=None):
    nc = core.nc
    last_layer = out is not None
    W = 4
    sem = lambda name, n=None: core.sem(f"{tag}_{name}", n)
    const_ld, x_ld, o_ld = sem("const_loaded"), sem("x_loaded", W), sem("rows_loaded", W)
    ix_ready, gath, step = sem("idx_ready"), sem("gathers"), sem("dve_step")
    summed, squares, std, eps_set = sem("summed"), sem("squares"), sem("std"), sem("eps_set")
    x_st, hn_ready, tp, t_out, t_st = sem("x_stored", W), sem("hn_ready", W), sem("transposed"), sem("hT_out", W), sem("hT_stored", W)
    with ExitStack() as ctx:
        sb = lambda name, shape, dt=F32: core.sb(ctx, f"{tag}_{name}", shape, dt)
        sbs = lambda name, n, shape, dt=F32: core.sbs(ctx, f"{tag}_{name}", n, shape, dt)
        gain, shift, scale = sb("gain", [P, D]), sb("shift", [P, D]), sb("scale", [P, D])
        ix = [sbs(f"idx{s}_", 2, [P, 1], I32) for s in range(W)]
        og = [sbs(f"rows{s}_", 2, [P, D]) for s in range(W)]
        xb, hn = sbs("x", W, [P, D]), sbs("hn", W, [P, D])
        junk = sb("junk", [P, D])
        eps = sb("eps", [P, 1])
        stat = sbs("stat", W, [P, 4])
        hT = sbs("hT", W, [P, KD, P])
        pT = [core.ps(ctx, f"{tag}_pT{s}", [P, KD, P]) for s in range(W)]
        block = ctx.enter_context(nc.Block())
        x1_view = x1_dram.rearrange("(n p) d -> n p d", p=P)
        if last_layer:
            out_view = out.rearrange("b (n p) d -> n p (b d)", p=P)
        else:
            x2_view = x2_dram.rearrange("(n p) d -> n p d", p=P)
            hT_view = hnT_dram.rearrange("(k p) (n f) -> n p k f", p=P, f=P)
        tile_of = lambda view, i, s: view[bass.ds(W * i + s, 1)].squeeze(0)

        @block.sync
        def _(sp):
            def load(i, s):
                sp.dma_start(xb[s][:], tile_of(x1_view, i, s)).then_inc(x_ld[s], 16)

            def store(i, s):
                sp.wait_ge(hn_ready[s], i + 1)
                if last_layer:
                    sp.dma_start(tile_of(out_view, i, s), hn[s][:]).then_inc(x_st[s], 16)
                else:
                    sp.dma_start(tile_of(x2_view, i, s), xb[s][:]).then_inc(x_st[s], 16)
                    sp.wait_ge(t_out[s], i + 2)
                    sp.dma_start(tile_of(hT_view, i, s), hT[s][:]).then_inc(t_st[s], 16)

            sp.dma_start(gain[:], row(gain_src, 0, D)).then_inc(const_ld, 16)
            if not last_layer:
                load_mod(sp, mod_dram, layer + 1, SC1, scale[:], const_ld)
                load_mod(sp, mod_dram, layer + 1, SH1, shift[:], const_ld)
            for s in range(W):
                load(0, s)
            with sp.Fori(0, NT // W - 1) as i:
                for s in range(W):
                    store(i, s)
                    sp.wait_ge(x_st[s], 16 * i + 16)
                    load(i + 1, s)
            for s in range(W):
                store(NT // W - 1, s)
            for s in range(W):
                sp.wait_ge(x_st[s], 16 * (NT // W))
                if not last_layer:
                    sp.wait_ge(t_st[s], 16 * (NT // W))

        @block.gpsimd
        def _(pool):
            with pool.Fori(0, NT // W) as i:
                for s in range(W):
                    n = W * i + s
                    pool.wait_ge(summed, n + 1)
                    for k in range(2):
                        pool.tensor_copy(ix[s][k][:], pos[:, bass.ds(n, 1), k]).then_inc(ix_ready, 1)
                    pool.wait_ge(ix_ready, 2 * n + 2)
                    pool.sem_inc(gath, 1)
                    for k in range(2):
                        pool.indirect_dma_start(og[s][k][:], None, o_dram,
                                                bass.IndirectOffsetOnAxis(ap=ix[s][k][:, 0:1], axis=0)) \
                            .then_inc(o_ld[s], 16)

        @block.scalar
        def _(act):
            if not last_layer:
                for s in range(W):
                    act.sem_inc(t_out[s], 1)

            def std_of(i, s):
                n = W * i + s
                act.wait_ge(summed, n + W + 1)
                act.activation(junk[:], xb[s][:], ACT.Square, accum_out=stat[s][:, 0:1]).then_inc(squares, 1)
                act.wait_ge(squares, n + 1)
                act.activation(stat[s][:, 1:2], stat[s][:, 0:1], ACT.Sqrt, scale=1.0 / D, bias=eps[:, 0:1]) \
                   .then_inc(std, 1)

            def out_t(i, s):
                act.wait_ge(tp, W * i + s + W + 1)
                if not (isinstance(i, int) and i == 0):
                    act.wait_ge(t_st[s], 16 * i)
                act.activation(hT[s][:], pT[s][:], ACT.Copy).then_inc(t_out[s], 1)

            act.wait_ge(eps_set, 1)
            def body(i, first, last):
                for s in range(W):
                    std_of(i, s)
                    if not last_layer and not (first and s == 0):
                        out_t(*at(i, s, -1, W))
            pairs(act, NT // W, body)
            if not last_layer:
                out_t(NT // W - 1, W - 1)

        if not last_layer:
            @block.tensor
            def _(pe):
                pe.sem_inc(tp, W)
                with pe.Fori(0, NT // W) as i:
                    for s in range(W):
                        pe.wait_ge(hn_ready[s], i + 1)
                        pe.wait_ge(t_out[s], i + 1)
                        for k in range(KD):
                            last = pe.transpose(pT[s][:, k, :], hn[s][:, k * P:(k + 1) * P], ident[:])
                        last.then_inc(tp, 1)

        @block.vector
        def _(dve):
            dve.memset(eps[:], EPS).then_inc(eps_set, 1)
            dve.wait_ge(const_ld, 16 if last_layer else 48)
            c = Chain(dve, step)
            if not last_layer:
                fold_scale(dve, c, gain[:], scale[:])
            base = c.n
            dve.sem_inc(summed, W)
            stt, tt = dve.scalar_tensor_tensor, dve.tensor_tensor
            steps = 2 if last_layer else 3

            def add(i, s):
                n = W * i + s
                c = Chain(dve, step, base + (steps * n - (steps - 1) if not isinstance(n, int) or n else 0))
                dve.wait_ge(x_ld[s], 16 * i + 16)
                dve.wait_ge(o_ld[s], 32 * i + 32)
                c(stt(out=xb[s][:], in0=og[s][0][:], scalar=wts[:, bass.ds(n, 1), 0], in1=xb[s][:],
                      op0=ALU.mult, op1=ALU.add))
                stt(out=xb[s][:], in0=og[s][1][:], scalar=wts[:, bass.ds(n, 1), 1], in1=xb[s][:],
                    op0=ALU.mult, op1=ALU.add).then_inc(summed, 1)

            def norm(i, s):
                n = W * i + s
                c = Chain(dve, step, base + steps * n + (1 if lastcall[0] else 2))
                dve.wait_ge(std, n + 1)
                if last_layer:
                    if not (isinstance(i, int) and i == 0):
                        dve.wait_ge(x_st[s], 16 * i)
                else:
                    dve.wait_ge(tp, n + 1)
                c(dve.reciprocal(stat[s][:, 2:3], stat[s][:, 1:2]))
                if last_layer:
                    stt(out=hn[s][:], in0=xb[s][:], scalar=stat[s][:, 2:3], in1=gain[:],
                        op0=ALU.mult, op1=ALU.mult).then_inc(hn_ready[s], 1)
                else:
                    c(stt(out=hn[s][:], in0=xb[s][:], scalar=stat[s][:, 2:3], in1=gain[:],
                          op0=ALU.mult, op1=ALU.mult))
                    tt(hn[s][:], hn[s][:], shift[:], ALU.add).then_inc(hn_ready[s], 1)

            lastcall = [False]
            add(0, 0)

            def body(i, first, last):
                for s in range(W):
                    if last and s == W - 1:
                        lastcall[0] = True
                    else:
                        add(*at(i, s, 1, W))
                    norm(i, s)
            pairs(dve, NT // W, body)


def conv_in(core, tag, w_in, conv_w, hnT_dram, z_dram):
    nc = core.nc
    NC_, MC = 4, 2
    W = P * MC
    TB = T // HALF
    sem = lambda name, n=None: core.sem(f"{tag}_{name}", n)
    w_ld = [sem(f"w{s}_loaded", KD) for s in range(2)]
    w_hi_r, w_split, cw_ld = sem("w_hi"), sem("w_split"), sem("taps_loaded")
    r_ld, r_hi, r_lo = sem("r_loaded", 2), sem("r_hi"), sem("r_split")
    mm, c_out, used, step = sem("bank"), sem("c_out"), sem("banks_read"), sem("dve_step")
    z_ready, z_go, z_st = sem("z_ready"), sem("z_stores"), sem("z_stored", 2)
    with ExitStack() as ctx:
        sb = lambda name, shape, dt=F32: core.sb(ctx, f"{tag}_{name}", shape, dt)
        sbs = lambda name, n, shape, dt=F32: core.sbs(ctx, f"{tag}_{name}", n, shape, dt)
        w_raw, w_lo = zip(*[core.raw_low(ctx, f"{tag}_w{s}", [P, KD, 3, W]) for s in range(2)])
        x_raw, x_lo = zip(*[core.raw_low(ctx, f"{tag}_x{s}", [P, KD, HALF]) for s in range(2)])
        w_hi, x_hi = sbs("w_hi", 2, [P, KD, 3, W], F32R), sbs("x_hi", 2, [P, KD, HALF], F32R)
        taps = sb("taps", [P, 3, NC_ * MC])
        u = sbs("u", 2, [P, MC, HALF + 2])
        cs = sbs("c", MC, [P, HALF])
        z = sbs("z", MC, [P, HALF])
        pb = [[core.ps(ctx, f"{tag}_p{j}_{m}", [P, HALF]) for j in range(3)] for m in range(MC)]
        block = ctx.enter_context(nc.Block())
        w_view = w_in[0].rearrange("(k p) (j c f) -> c p k j f", p=P, j=3, f=W)
        x_view = hnT_dram.rearrange("(k p) (n f) -> n p k f", p=P, f=HALF)
        z_view = z_dram.rearrange("(c p) (n f) -> c n p f", p=P, f=HALF)

        @block.sync
        def _(sp):
            def weights(c):
                for k in range(KD):
                    sp.dma_start(w_raw[c % 2][:, k, :, :], w_view[c][:, k, :, :]).then_inc(w_ld[c % 2][k], 16)

            def load(r, t, s):
                sp.dma_start(x_raw[s][:], x_view[bass.ds(t, 1)].squeeze(0)).then_inc(r_ld[s], 16)

            sp.dma_start(taps[:], conv_w[0].rearrange("j (c p) -> p j c", p=P), allow_slow_non_contiguous=True) \
              .then_inc(cw_ld, 16)
            weights(0)
            for s in range(2):
                load(0, s, s)
            for c in range(NC_):
                if c + 1 < NC_:
                    if c >= 1:
                        sp.wait_ge(mm, 3 * MC * TB * c)
                    weights(c + 1)
                last = c == NC_ - 1
                with sp.Fori(0, TB // 2 - (1 if last else 0)) as i:
                    for s in range(2):
                        b = c * TB + 2 * i + s
                        sp.wait_ge(mm, 3 * MC * (b + 1))
                        load(None, (2 * i + s + 2) % TB, s)

        @block.scalar
        def _(act):
            def split_w(c):
                for k in range(KD):
                    act.wait_ge(w_ld[c % 2][k], 16 * (c // 2 + 1))
                    act.activation(w_hi[c % 2][:, k, :, :], w_raw[c % 2][:, k, :, :], ACT.Copy) \
                       .then_inc(w_hi_r, 1)

            def split_x(c, i, s):
                b = c * TB + 2 * i + s
                act.wait_ge(r_ld[s], 16 * (c * (TB // 2) + i + 1))
                if not isinstance(b, int) or b >= 2:
                    act.wait_ge(mm, 3 * MC * (b - 1))
                for h in range(2):
                    act.activation(x_hi[s][:, 4 * h:4 * h + 4, :], x_raw[s][:, 4 * h:4 * h + 4, :],
                                   ACT.Copy).then_inc(r_hi, 1)

            split_w(0)
            split_x(0, 0, 0)
            for c in range(NC_):
                if c + 1 < NC_:
                    split_w(c + 1)

                def body(i, first, last):
                    for s in range(2):
                        b = c * TB + 2 * i + s
                        if not (c == NC_ - 1 and last and s == 1):
                            split_x(c, *at(i, s, 1))
                        for m in range(MC):
                            act.wait_ge(mm, 3 * (MC * b + m) + 1)
                            act.wait_ge(used, MC * b + 1 + m)
                            act.activation(cs[m][:], pb[m][0][:], ACT.Copy).then_inc(c_out, 1)
                pairs(act, TB // 2, body)

        @block.tensor
        def _(pe):
            for c in range(NC_):
                pe.wait_ge(w_split, KD * (c + 1))
                with pe.Fori(0, TB // 2) as i:
                    for s in range(2):
                        b = c * TB + 2 * i + s
                        pe.wait_ge(r_lo, 2 * b + 2)
                        for m in range(MC):
                            pe.wait_ge(used, MC * b + 1 + m)
                            for n, j in enumerate((1, 2, 0)):
                                cols = slice(m * P, (m + 1) * P)
                                for k in range(KD):
                                    last = product(pe, pb[m][n][:], (w_hi[c % 2][:, k, j, cols], w_lo[c % 2][:, k, j, cols]),
                                                   (x_hi[s][:, k, :], x_lo[s][:, k, :]), k == 0, k == KD - 1)
                                last.then_inc(mm, 1)

        @block.gpsimd
        def _(pool):
            for c in range(NC_):
                with pool.Fori(0, TB) as n:
                    for m in range(MC):
                        b = c * TB + n
                        pool.wait_ge(z_ready, MC * b + m + 1)
                        pool.sem_inc(z_go, 1)
                        pool.dma_start(z_view[MC * c + m][bass.ds(n, 1)].squeeze(0), z[m][:]).then_inc(z_st[m], 16)
            for m in range(MC):
                pool.wait_ge(z_st[m], 16 * NC_ * TB)

        @block.vector
        def _(dve):
            dve.sem_inc(used, 2)
            dve.wait_ge(cw_ld, 16)

            def split_w(c):
                for k in range(KD):
                    dve.wait_ge(w_hi_r, KD * c + k + 1)
                    dve.tensor_tensor(w_lo[c % 2][:, k, :, :], w_raw[c % 2][:, k, :, :], w_hi[c % 2][:, k, :, :].bitcast(F32), ALU.subtract) \
                       .then_inc(w_split, 1)

            def split_x(c, i, s):
                b = c * TB + 2 * i + s
                for h in range(2):
                    dve.wait_ge(r_hi, 2 * b + h + 1)
                    dve.tensor_tensor(x_lo[s][:, 4 * h:4 * h + 4, :], x_raw[s][:, 4 * h:4 * h + 4, :], x_hi[s][:, 4 * h:4 * h + 4, :].bitcast(F32), ALU.subtract) \
                       .then_inc(r_lo, 1)

            per = 5
            split_w(0)
            split_x(0, 0, 0)
            for c in range(NC_):
                if c + 1 < NC_:
                    split_w(c + 1)
                base = c * (TB * MC * per + 1)
                Chain(dve, step, base)(dve.memset(u[0][:, :, 0:2], 0.0))
                base += 1

                def body(i, first, last):
                    for s in range(2):
                        b = c * TB + 2 * i + s
                        if not (c == NC_ - 1 and last and s == 1):
                            split_x(c, *at(i, s, 1))
                        for m in range(MC):
                            q = Chain(dve, step, base + ((2 * i + s) * MC + m) * per)
                            tap = lambda j: taps[:, j, MC * c + m:MC * c + m + 1]
                            dve.wait_ge(mm, 3 * (MC * b + m) + 2)
                            dve.wait_ge(c_out, MC * b + m + 1)
                            q(dve.tensor_tensor(u[s][:, m, 2:], cs[m][:], pb[m][1][:], ALU.mult))
                            q(dve.tensor_copy(u[1 - s][:, m, 0:2], u[s][:, m, HALF:HALF + 2]))
                            if not isinstance(b, int) or b >= 1:
                                dve.wait_ge(z_st[m], 16 * b)
                            q(dve.tensor_scalar(z[m][:], u[s][:, m, 0:HALF], tap(0), None, ALU.mult))
                            q(dve.scalar_tensor_tensor(out=z[m][:], in0=u[s][:, m, 1:HALF + 1], scalar=tap(1), in1=z[m][:],
                                                       op0=ALU.mult, op1=ALU.add))
                            q(dve.scalar_tensor_tensor(out=z[m][:], in0=u[s][:, m, 2:], scalar=tap(2), in1=z[m][:],
                                                       op0=ALU.mult, op1=ALU.add))
                            dve.wait_ge(mm, 3 * (MC * b + m) + 3)
                            dve.tensor_tensor(z[m][:], z[m][:], pb[m][2][:], ALU.mult).then_inc(z_ready, 1)
                            dve.wait_ge(z_ready, MC * b + m + 1)
                            dve.sem_inc(used, 1)
                pairs(dve, TB // 2, body)



def program(nc, x, c, ada_w, ada_b, norm1_g, norm2_g, ssm_w_in, ssm_lam_re, ssm_lam_im, ssm_log_dt, ssm_b_re,
            ssm_b_im, ssm_c_re, ssm_c_im, ssm_d, ssm_w_glu, conv_w_in, conv_w, conv_w_out, moe_wg, moe_bg, moe_we,
            moe_be, moe_w1, moe_w3, moe_w2, final_g, out):
    dram = lambda name, shape, dt=F32: nc.dram_tensor(name, shape, dt).ap()
    mod = dram("mod", [2, MOD])
    u = dram("u", [G, P, L * CH])
    y, hn, hnT, zT = dram("y", [T, D]), dram("hn", [T, D]), dram("hnT", [D, T]), dram("zT", [D, T])
    x1, x2 = dram("x1", [T, D]), dram("x2", [T, D])
    o = dram("expert_rows", [TILES * P, D])
    slots = dram("slot_token", [SLOTS, 1], I32)
    rows = lambda a: a.rearrange("(n p) d -> n p d", p=P)
    with ExitStack() as ctx:
        core = Core(nc, ctx)
        ident = core.sb(ctx, "ident", [P, P])
        logits = core.sb(ctx, "logits", [P, NT, NL])
        pos, wts = core.sb(ctx, "pos", [P, NT, 2], I32), core.sb(ctx, "wts", [P, NT, 2])
        table = core.sb(ctx, "expert_table", [1, 2 * NE + 1], I32)

        def moe(layer):
            core.phase(routing, f"r{layer}", logits, pos, wts, table, slots,
                       *((1, c, ada_w, ada_b, mod) if layer == 0 else ()))
            core.phase(experts, ident, f"m{layer}", layer, moe_w1, moe_w3, moe_w2, mod, table, slots, hn, o)

        core.phase(constants, ident)
        with ExitStack() as ssm:
            tab = SsmTables(core, ssm)
            core.phase(ssm_tables, ident, ssm_lam_re, ssm_lam_im, ssm_log_dt, ssm_b_re, ssm_b_im, ssm_c_re, ssm_c_im,
                       ssm_d, tab, c, ada_w, ada_b, mod)
            core.phase(ssm_input, ident, x, norm1_g, ssm_w_in, mod, u)
            core.phase(ssm_scan, ident, tab, u, y)
        core.phase(project, ident, "glu", 0, True, y, ssm_w_glu[0], x.rearrange("b (n p) d -> n p (b d)", p=P), norm2_g,
                moe_wg, moe_bg, moe_we, moe_be, mod, x1, hn, logits)
        moe(0)
        core.phase(combine, ident, "c0", 0, pos, wts, o, x1, mod, norm1_g[1:2, :], x2_dram=x2, hnT_dram=hnT)
        core.phase(conv_in, "conv", conv_w_in, conv_w, hnT, zT)
        core.phase(project, ident, "cout", 1, False, zT, conv_w_out[0], rows(x2), norm2_g,
                moe_wg, moe_bg, moe_we, moe_be, mod, x1, hn, logits)
        moe(1)
        core.phase(combine, ident, "c1", 1, pos, wts, o, x1, mod, final_g.rearrange("(a d) -> a d", a=1), out=out)


_INS = ["x", "c", "ada_w", "ada_b", "norm1_g", "norm2_g", "ssm_w_in", "ssm_lam_re", "ssm_lam_im", "ssm_log_dt",
        "ssm_b_re", "ssm_b_im", "ssm_c_re", "ssm_c_im", "ssm_d", "ssm_w_glu", "conv_w_in", "conv_w", "conv_w_out",
        "moe_wg", "moe_bg", "moe_we", "moe_be", "moe_w1", "moe_w3", "moe_w2", "final_g"]
_OUTS = [((1, T, D), "float32")]


def kernel(**inputs):
    import numpy as _np
    import concourse.bacc as _bacc
    from concourse import mybir as _mybir
    from concourse.bass_utils import run_bass_kernel_spmd as _run

    nc = _bacc.Bacc("TRN2", target_bir_lowering=False, num_devices=1)
    arrays, args = {}, []
    for name in _INS:
        a = _np.ascontiguousarray(inputs[name])
        arrays[f"in_{name}_dram"] = a
        args.append(nc.dram_tensor(f"in_{name}_dram", a.shape, _mybir.dt.from_np(a.dtype), kind="ExternalInput").ap())
    for i, (shape, dtype) in enumerate(_OUTS):
        dt = _mybir.dt.from_np(_np.dtype(dtype))
        args.append(nc.dram_tensor(f"out_{i}_dram", shape, dt, kind="ExternalOutput").ap())
    program(nc, *args)
    r = _run(nc, [arrays], core_ids=[0])
    return r.results[0]["out_0_dram"]
```
